# Optimizing a Trainium2 kernel written in Bass

```python
import math
import jax, jax.numpy as jnp
from jax import lax
import numpy as np

D_MODEL = 1024
BATCH = 1
SEQ = 512
DEPTH = 2

N_MIXERS = 4
EXPAND = 2
D_INNER = EXPAND * D_MODEL
NORM_EPS = 1e-6
ROPE_THETA = 10000.0
Q_BLOCK = 128

A_HEADS = 16
A_HEAD_DIM = D_INNER // A_HEADS
A_IDX_HEADS = 16
A_IDX_DIM = 64
A_TOPK_MAX = 256
A_SPLITS = (A_HEADS * A_HEAD_DIM, A_HEAD_DIM, A_HEAD_DIM, A_IDX_HEADS * A_IDX_DIM, A_IDX_DIM, A_IDX_HEADS, D_INNER)

B_HEADS = 16
B_HEAD_DIM = D_INNER // B_HEADS
B_CONFIGS = ((128, 1), (512, 4), (2048, 16))

C_HEADS = 8
C_QK_DIM = D_MODEL // C_HEADS
C_V_DIM = D_INNER // C_HEADS
C_CHUNK = 128
C_SPLITS = (C_HEADS * C_QK_DIM, C_HEADS * C_QK_DIM, D_INNER, D_INNER)

D_HEADS = 16
D_K_DIM = D_INNER // D_HEADS
D_V_DIM = D_INNER // D_HEADS
D_CHUNK = 64

kernel_name = "hybrid_dsa_dilated_retnet_hgrn2_trunk"

def _n_layers_of(kind):
    return len(range(kind, DEPTH, N_MIXERS))

def rmsnorm(x, g):
    x32 = x.astype(jnp.float32)
    y = x32 * lax.rsqrt(jnp.mean(x32 * x32, axis=-1, keepdims=True) + NORM_EPS)
    return (y * g.astype(jnp.float32)).astype(x.dtype)

def head_rmsnorm(x):
    x32 = x.astype(jnp.float32)
    return x32 * lax.rsqrt(jnp.mean(x32 * x32, axis=-1, keepdims=True) + NORM_EPS)

def rotary(x, pos):
    dh = x.shape[-1]
    freqs = ROPE_THETA ** (-jnp.arange(0, dh, 2, dtype=jnp.float32) / dh)
    ang = pos.astype(jnp.float32)[:, None] * freqs[None, :]
    cos = jnp.cos(ang)[:, None, :].astype(x.dtype)
    sin = jnp.sin(ang)[:, None, :].astype(x.dtype)
    x1, x2 = jnp.split(x, 2, axis=-1)
    return jnp.concatenate([x1 * cos - x2 * sin, x1 * sin + x2 * cos], axis=-1)

def _split(t, sizes):
    return jnp.split(t, np.cumsum(sizes)[:-1].tolist(), axis=-1)

def dsa_mixer(h, w_in, w_out):
    B_, S, _ = h.shape
    pos = jnp.arange(S)
    q, k, v, iq, ik, iw, z = _split(h @ w_in, A_SPLITS)
    q = rotary(q.reshape(B_, S, A_HEADS, A_HEAD_DIM), pos) * (A_HEAD_DIM ** -0.5)
    k = rotary(k.reshape(B_, S, 1, A_HEAD_DIM), pos)[:, :, 0]
    iq = rotary(iq.reshape(B_, S, A_IDX_HEADS, A_IDX_DIM), pos)
    ik = rotary(ik.reshape(B_, S, 1, A_IDX_DIM), pos)[:, :, 0]
    iw = iw * (A_IDX_HEADS ** -0.5 * A_IDX_DIM ** -0.5)
    top_k = min(A_TOPK_MAX, S // 4)
    nb = S // Q_BLOCK

    def blockify(t):
        return t.reshape(B_, nb, Q_BLOCK, *t.shape[2:]).swapaxes(0, 1)

    def one_block(args):
        qb, iqb, iwb, tb = args
        rel = jax.nn.relu(jnp.einsum('bqhd,bsd->bqsh', iqb, ik))
        score = jnp.einsum('bqsh,bqh->bqs', rel, iwb).astype(jnp.float32)
        causal = pos[None, None, :] <= tb[None, :, None]
        score = jnp.where(causal, score, -jnp.inf)
        _, sel = lax.top_k(score, top_k)
        valid = sel <= tb[None, :, None]
        k_sel = jax.vmap(lambda kk, ii: kk[ii])(k, sel)
        v_sel = jax.vmap(lambda vv, ii: vv[ii])(v, sel)
        s = jnp.einsum('bqhd,bqkd->bhqk', qb, k_sel).astype(jnp.float32)
        s = jnp.where(valid[:, None], s, -jnp.inf)
        p = jax.nn.softmax(s, axis=-1).astype(v.dtype)
        return jnp.einsum('bhqk,bqkd->bqhd', p, v_sel)

    tpos = pos.reshape(nb, Q_BLOCK)
    o = lax.map(one_block, (blockify(q), blockify(iq), blockify(iw), tpos))
    o = o.swapaxes(0, 1).reshape(B_, S, D_INNER)
    return (o * jax.nn.silu(z)) @ w_out

def _dilated_band_attention(q, k, v, window, dilation):
    B_, S, H, dh = q.shape
    L = S // dilation
    span = window // dilation
    blk = Q_BLOCK
    nb = -(-L // blk)
    Lp = nb * blk

    def residues(t):
        t = t.reshape(B_, L, dilation, H, dh).transpose(0, 2, 1, 3, 4)
        return jnp.pad(t, ((0, 0), (0, 0), (0, Lp - L), (0, 0), (0, 0)))

    def band(t):
        tp = jnp.pad(t, ((0, 0), (0, 0), (blk, 0), (0, 0), (0, 0))).reshape(B_, dilation, nb + 1, blk, H, dh)
        return jnp.concatenate([tp[:, :, :-1], tp[:, :, 1:]], axis=3)

    qb = residues(q).reshape(B_, dilation, nb, blk, H, dh)
    kb, vb = band(residues(k)), band(residues(v))
    s = jnp.einsum('brnqhd,brnkhd->brnqhk', qb, kb).astype(jnp.float32)
    qi = jnp.arange(blk)[:, None]
    ki = jnp.arange(2 * blk)[None, :]
    dist = blk + qi - ki
    key_m = jnp.arange(nb)[:, None, None] * blk - blk + ki[None]
    valid = (dist >= 0)[None] & (dist <= span)[None] & (key_m >= 0)
    s = jnp.where(valid[:, :, None, :], s, -jnp.inf)
    m = jnp.max(s, axis=-1, keepdims=True)
    p = jnp.exp(s - m)
    den = jnp.sum(p, axis=-1, keepdims=True)
    o = jnp.einsum('brnqhk,brnkhd->brnqhd', (p / den).astype(v.dtype), vb)
    lse = (m + jnp.log(den))[..., 0]
    o = o.reshape(B_, dilation, Lp, H, dh)[:, :, :L].transpose(0, 2, 1, 3, 4).reshape(B_, S, H, dh)
    lse = lse.reshape(B_, dilation, Lp, H)[:, :, :L].transpose(0, 2, 1, 3).reshape(B_, S, H)
    return o, lse

def dilated_mixer(h, w_in, w_out):
    B_, S, _ = h.shape
    pos = jnp.arange(S)
    q, k, v, z = jnp.split(h @ w_in, 4, axis=-1)
    q = rotary(q.reshape(B_, S, B_HEADS, B_HEAD_DIM), pos) * (B_HEAD_DIM ** -0.5)
    k = rotary(k.reshape(B_, S, B_HEADS, B_HEAD_DIM), pos)
    v = v.reshape(B_, S, B_HEADS, B_HEAD_DIM)
    outs, lses = [], []
    for window, dilation in B_CONFIGS:
        o_g, lse_g = _dilated_band_attention(q, k, v, window, dilation)
        outs.append(o_g.astype(jnp.float32))
        lses.append(lse_g)
    alpha = jax.nn.softmax(jnp.stack(lses), axis=0)
    o = jnp.einsum('gbsh,gbshd->bshd', alpha, jnp.stack(outs)).astype(h.dtype).reshape(B_, S, D_INNER)
    return (o * jax.nn.silu(z)) @ w_out

def retention_mixer(h, w_in, w_out):
    B_, S, _ = h.shape
    pos = jnp.arange(S)
    q, k, v, z = _split(h @ w_in, C_SPLITS)
    q = rotary(q.reshape(B_, S, C_HEADS, C_QK_DIM), pos).astype(jnp.float32)
    k = (rotary(k.reshape(B_, S, C_HEADS, C_QK_DIM), pos) * (C_QK_DIM ** -0.5)).astype(jnp.float32)
    v = v.reshape(B_, S, C_HEADS, C_V_DIM).astype(jnp.float32)
    log_gamma = jnp.log1p(-jnp.exp2(-5.0 - jnp.arange(C_HEADS, dtype=jnp.float32)))
    n = S // C_CHUNK
    qc = q.reshape(B_, n, C_CHUNK, C_HEADS, C_QK_DIM)
    kc = k.reshape(B_, n, C_CHUNK, C_HEADS, C_QK_DIM)
    vc = v.reshape(B_, n, C_CHUNK, C_HEADS, C_V_DIM)
    idx = jnp.arange(C_CHUNK, dtype=jnp.float32)
    rel = idx[:, None] - idx[None, :]
    decay = jnp.where(rel[None] >= 0, jnp.exp(jnp.maximum(rel, 0.0)[None] * log_gamma[:, None, None]), 0.0)
    scores = jnp.einsum('bnihd,bnjhd->bnhij', qc, kc) * decay
    o_intra = jnp.einsum('bnhij,bnjhe->bnihe', scores, vc)
    k_decay = jnp.exp((C_CHUNK - 1 - idx)[None, :] * log_gamma[:, None])
    kv = jnp.einsum('bnjhd,hj,bnjhe->bnhde', kc, k_decay, vc)
    chunk_decay = jnp.exp(C_CHUNK * log_gamma)[:, None, None]

    def step(state, kv_n):
        return state * chunk_decay + kv_n, state

    _, prev = lax.scan(step, jnp.zeros((B_, C_HEADS, C_QK_DIM, C_V_DIM), jnp.float32), kv.swapaxes(0, 1))
    prev = prev.swapaxes(0, 1)
    q_decay = jnp.exp((idx + 1.0)[None, :] * log_gamma[:, None])
    o_inter = jnp.einsum('bnihd,hi,bnhde->bnihe', qc, q_decay, prev)
    o = head_rmsnorm((o_intra + o_inter).reshape(B_, S, C_HEADS, C_V_DIM))
    o = o.reshape(B_, S, D_INNER).astype(h.dtype)
    return (o * jax.nn.silu(z)) @ w_out

def hgrn2_mixer(h, w_in, w_out, lower_bound):
    B_, S, _ = h.shape
    q, f, i, z = jnp.split(h @ w_in, 4, axis=-1)
    q = jax.nn.silu(q.astype(jnp.float32)) * (D_K_DIM ** -0.5)
    g = lower_bound + (1.0 - lower_bound) * jax.nn.sigmoid(f.astype(jnp.float32))
    log_f = jnp.log(g)
    k = 1.0 - g
    n = S // D_CHUNK

    def chunks(t, d):
        return t.reshape(B_, n, D_CHUNK, D_HEADS, d).swapaxes(0, 1)

    qs, ks, ls = chunks(q, D_K_DIM), chunks(k, D_K_DIM), chunks(log_f, D_K_DIM)
    vs = chunks(i.astype(jnp.float32), D_V_DIM)
    tri = jnp.arange(D_CHUNK)[:, None] >= jnp.arange(D_CHUNK)[None, :]

    def step(state, inp):
        qn, kn, vn, ln = inp
        b = jnp.cumsum(ln, axis=1)
        diff = jnp.where(tri[None, :, :, None, None], b[:, :, None] - b[:, None, :], -jnp.inf)
        a = jnp.einsum('bthk,bshk,btshk->bhts', qn, kn, jnp.exp(diff))
        o = jnp.einsum('bhts,bshv->bthv', a, vn) + jnp.einsum('bthk,bhkv->bthv', qn * jnp.exp(b), state)
        b_last = b[:, -1]
        new_state = state * jnp.exp(b_last)[..., None] + jnp.einsum('bshk,bshv->bhkv', kn * jnp.exp(b_last[:, None] - b), vn)
        return new_state, o

    _, o = lax.scan(step, jnp.zeros((B_, D_HEADS, D_K_DIM, D_V_DIM), jnp.float32), (qs, ks, vs, ls))
    o = head_rmsnorm(o.swapaxes(0, 1).reshape(B_, S, D_HEADS, D_V_DIM))
    o = o.reshape(B_, S, D_INNER).astype(h.dtype)
    return (o * jax.nn.silu(z)) @ w_out

def setup_inputs(seed: int = 0) -> dict:
    key = jax.random.key(seed)
    ks = jax.random.split(key, 13)
    a_cols = sum(A_SPLITS)
    c_cols = sum(C_SPLITS)
    na, nb_, nc, nd = (_n_layers_of(m) for m in range(N_MIXERS))

    def w(k, shape, fan_in):
        return jax.random.normal(k, shape, jnp.float32) * (fan_in ** -0.5)

    return {
        "x": jax.random.normal(ks[0], (BATCH, SEQ, D_MODEL), jnp.float32),
        "norm_g": 1.0 + 0.02 * jax.random.normal(ks[1], (DEPTH, D_MODEL), jnp.float32),
        "final_g": 1.0 + 0.02 * jax.random.normal(ks[2], (D_MODEL,), jnp.float32),
        "a_w_in": w(ks[3], (na, D_MODEL, a_cols), D_MODEL),
        "a_w_out": w(ks[4], (na, D_INNER, D_MODEL), D_INNER),
        "b_w_in": w(ks[5], (nb_, D_MODEL, 4 * D_INNER), D_MODEL),
        "b_w_out": w(ks[6], (nb_, D_INNER, D_MODEL), D_INNER),
        "c_w_in": w(ks[7], (nc, D_MODEL, c_cols), D_MODEL),
        "c_w_out": w(ks[8], (nc, D_INNER, D_MODEL), D_INNER),
        "d_w_in": w(ks[9], (nd, D_MODEL, 4 * D_INNER), D_MODEL),
        "d_w_out": w(ks[10], (nd, D_INNER, D_MODEL), D_INNER),
        "hgrn_lb_logits": 0.5 * jax.random.normal(ks[11], (DEPTH, D_INNER), jnp.float32),
    }

def reference(x, norm_g, final_g, a_w_in, a_w_out, b_w_in, b_w_out, c_w_in, c_w_out, d_w_in, d_w_out, hgrn_lb_logits):
    lb_cum = jnp.cumsum(jax.nn.softmax(hgrn_lb_logits.astype(jnp.float32), axis=0), axis=0)
    lower_bounds = lb_cum - lb_cum[0]
    h = x
    for layer in range(DEPTH):
        kind = layer % N_MIXERS
        slot = layer // N_MIXERS
        u = rmsnorm(h, norm_g[layer])
        if kind == 0:
            y = dsa_mixer(u, a_w_in[slot], a_w_out[slot])
        elif kind == 1:
            y = dilated_mixer(u, b_w_in[slot], b_w_out[slot])
        elif kind == 2:
            y = retention_mixer(u, c_w_in[slot], c_w_out[slot])
        else:
            y = hgrn2_mixer(u, d_w_in[slot], d_w_out[slot], lower_bounds[layer])
        h = h + y
    return rmsnorm(h, final_g)


_drawn_inputs = setup_inputs


def setup_inputs(seed=0):
    import zlib

    import numpy as np

    out = dict(_drawn_inputs(seed))
    spreads = {}
    factors = {'norm_g': 4.63, 'final_g': 2.786}
    for name, (base, spread) in spreads.items():
        noise = np.random.default_rng([zlib.crc32(name.encode()), seed]).standard_normal(out[name].shape)
        drawn = base * np.exp(spread * noise) if base else spread * noise
        out[name] = __import__('jax').numpy.asarray(drawn.astype(out[name].dtype))
    for name, factor in factors.items():
        out[name] = (out[name] * factor).astype(out[name].dtype)
    return out
```

```python
from contextlib import ExitStack

import numpy as np

import concourse.bass as bass
from concourse import mybir

F32 = mybir.dt.float32
F32R = mybir.dt.float32r
ALU = mybir.AluOpType
ACT = mybir.ActivationFunctionType

P = 128
D_MODEL, SEQ, D_INNER = 1024, 512, 2048
KT = D_MODEL // P
QB = SEQ // P
HEADS, HEAD_DIM = 16, 128
IDX_HEADS, IDX_DIM = 16, 64
IDX_TILES = IDX_HEADS * IDX_DIM // P
TOP_K = min(256, SEQ // 4)
NORM_EPS = 1e-6
SCALE = HEAD_DIM ** -0.5
IDX_SCALE = IDX_HEADS ** -0.5 * IDX_DIM ** -0.5
NEG = -3e38
CONFIGS = ((128, 1), (512, 4), (2048, 16))

OFF = [P * i * (i + 1) // 2 for i in range(QB)]
COLS = P * QB * (QB + 1) // 2
T_OFF = [0, SEQ, SEQ + 3 * P, SEQ + 5 * P]

T_IK, T_IQ, T_V, T_K, T_Z = 0, 1, 1 + IDX_TILES, 2 + IDX_TILES, 3 + IDX_TILES
LATE_GATES = 2
EARLY_GATES = HEADS - LATE_GATES
T_Q = T_Z + EARLY_GATES
T_LATE = T_Q + HEADS
T_OUT = [T_LATE + LATE_GATES, T_LATE + LATE_GATES + HEADS + 4 * HEADS]
T_B = T_OUT[0] + HEADS
TILES = T_OUT[1] + HEADS
PROJ_B = T_OUT[0]
R_IQ, R_K = 1, 1 + IDX_TILES
R_Q = R_K + 1
R_B = R_Q + HEADS
assert TOP_K == P and T_OFF[-1] + P == COLS

M_ORDER = (0, 1, 2, 3, 4, 6, 7, 5)
S_BANK, T_BANK = 2, 5


class Count:

    def __init__(self, base, per=0, turn=None):
        self.base, self.per, self.turn = base, per, turn

    def __add__(self, k):
        return Count(self.base + k, self.per, self.turn)

    def __sub__(self, k):
        return self + (-k)

    def __mul__(self, k):
        return Count(self.base * k, self.per * k, self.turn)

    @property
    def value(self):
        return self.turn * self.per + self.base if self.per else self.base

    @property
    def slot(self):
        assert self.per % 2 == 0
        return self.base % 2

    @property
    def half(self):
        assert self.per % 2 == 0
        return Count(self.base // 2, self.per // 2, self.turn)


def number(count):
    return count.value if isinstance(count, Count) else count


def above_zero(count):
    return (count.base if isinstance(count, Count) else count) > 0


def in_register(eng, count):
    return eng.to_reg(count.value) if count.per else count.base


def build(nc, xT, gains, weights, rope_tables, dilated_bias, causal_bias, ident_in, outT):
    with ExitStack() as ctx:
        def sb(name, shape, dt=F32):
            return ctx.enter_context(nc.sbuf_tensor(name, shape, dt))

        def sem(name):
            return ctx.enter_context(nc.semaphore(name))

        ps = ctx.enter_context(nc.psum_tensor("ps", [P, 8, SEQ], F32))

        w_raw = sb("w_raw", [P, 2, D_MODEL])
        w_hi = sb("w_hi", [P, 2, D_MODEL], F32R)
        w_lo = sb("w_lo", [P, 2, D_MODEL], F32R)
        h = sb("h", [P, KT, SEQ])
        u_hi = sb("u_hi", [P, KT, SEQ], F32R)
        u_lo = sb("u_lo", [P, KT, SEQ], F32R)
        u_f = sb("u_f", [P, 4, SEQ])
        gain = sb("gain", [P, 3 * KT])
        square = sb("square", [P, 2, SEQ])
        rstd = sb("rstd", [P, SEQ])
        ones = sb("ones", [P, P])
        ident = sb("ident", [P, P])
        table = sb("table", [P, 4, SEQ])
        by_cos = sb("by_cos", [P, SEQ])
        by_sin = sb("by_sin", [P, SEQ])
        rotated = sb("rotated", [P, 2, SEQ])
        q_hi = sb("q_hi", [P, 2, SEQ], F32R)
        q_lo = sb("q_lo", [P, 2, SEQ], F32R)
        k_hi = sb("k_hi", [P, SEQ], F32R)
        k_lo = sb("k_lo", [P, SEQ], F32R)
        v_f = sb("v_f", [P, SEQ])
        v_hi = sb("v_hi", [P, SEQ], F32R)
        v_lo = sb("v_lo", [P, SEQ], F32R)
        bias_a = sb("bias_a", [P, COLS])
        bias_b = sb("bias_b", [P, SEQ])
        neg_s = sb("neg_s", [P, COLS])
        neg_max = sb("neg_max", [P, QB])
        probs = sb("probs", [P, COLS])
        den = sb("den", [P, QB])
        inv_den = sb("inv_den", [P, QB])
        pT_hi = sb("pT_hi", [P, COLS], F32R)
        pT_lo = sb("pT_lo", [P, COLS], F32R)
        gated = sb("gated", [P, HEADS, SEQ])
        o_hi = sb("o_hi", [P, 2, SEQ], F32R)
        o_lo = sb("o_lo", [P, 2, SEQ], F32R)
        ik = sb("ik", [P, 4, SEQ], F32R)
        iwT = sb("iwT", [IDX_HEADS, SEQ])
        iw = sb("iw", [P, QB - 1, IDX_HEADS])
        rel = [neg_s[:, 0:COLS - P], probs[:, 0:COLS - P]]
        score = sb("score", [P, COLS - P])
        left = rel[0]
        top8 = sb("top8", [P, QB - 1, 8])

        x_landed = [sem(f"x_landed{m}") for m in range(KT)]
        gain_landed, table_landed, bias_landed = sem("gain_landed"), sem("table_landed"), sem("bias_landed")
        w_landed = [sem("w_landed0"), sem("w_landed1")]
        w_hi_ready, w_lo_ready, tile_done = sem("w_hi_ready"), sem("w_lo_ready"), sem("tile_done")
        ones_ready, squares_ready, squares_used = sem("ones_ready"), sem("squares_ready"), sem("squares_used")
        mean_ready, root_ready, rstd_ready = sem("mean_ready"), sem("root_ready"), sem("rstd_ready")
        u_ready, u_hi_ready = sem("u_ready"), sem("u_hi_ready")
        u_lo_pool, u_lo_dve = sem("u_lo_pool"), sem("u_lo_dve")
        bank_read = [sem("bank_read0"), sem("bank_read1")]
        rotated_ready = sem("rotated_ready")
        rope_hi_ready, rope_lo_ready = sem("rope_hi_ready"), sem("rope_lo_ready")
        ik_zeroed, iwT_ready, iw_turned, iw_ready = (
            sem("ik_zeroed"), sem("iwT_ready"), sem("iw_turned"), sem("iw_ready"))
        idx_done, rel_ready, score_ready = sem("idx_done"), sem("rel_ready"), sem("score_ready")
        score_zeroed, left_ready, top8_ready, top8_taken = (
            sem("score_zeroed"), sem("left_ready"), sem("top8_ready"), sem("top8_taken"))
        chosen_ready, bias_ready = sem("chosen_ready"), sem("bias_ready")
        v_turned, v_hi_ready, v_lo_ready = sem("v_turned"), sem("v_hi_ready"), sem("v_lo_ready")
        scores_done, scores_read, exp_done, inv_ready, probs_ready = (
            sem("scores_done"), sem("scores_read"), sem("exp_done"), sem("inv_ready"), sem("probs_ready"))
        probs_turned, pT_hi_ready, pT_lo_ready, o_done, gated_ready = (
            sem("probs_turned"), sem("pT_hi_ready"), sem("pT_lo_ready"), sem("o_done"), sem("gated_ready"))
        o_lo_ready, o_hi_ready, y_done, residual_ready = (
            sem("o_lo_ready"), sem("o_hi_ready"), sem("y_done"), sem("residual_ready"))
        out_stored = sem("out_stored")

        block = ctx.enter_context(nc.Block())

        @block.sync
        def _(sp):
            def load_tile(g):
                if above_zero(g - 1):
                    sp.wait_ge(w_lo_ready, number(g - 1))
                sp.dma_start(w_raw[:, g.slot, :], weights[g.value]).then_inc(w_landed[g.slot], 16)

            for m in range(KT // 2):
                sp.dma_start(h[:, m, :], xT[m * P:(m + 1) * P, :]).then_inc(x_landed[m], 16)
            load_tile(Count(0))
            for m in range(KT // 2, KT):
                sp.dma_start(h[:, m, :], xT[m * P:(m + 1) * P, :]).then_inc(x_landed[m], 16)
            load_tile(Count(1))
            with sp.Fori(0, TILES // 2 - 1) as i:
                load_tile(Count(2, 2, i))
                load_tile(Count(3, 2, i))
            for g in range(TILES // 2 * 2, TILES):
                load_tile(Count(g))
            for m in range(KT):
                sp.wait_ge(u_ready, number(2 * KT + m + 1))
                sp.dma_start(outT[m * P:(m + 1) * P, :], h[:, m, :]).then_inc(out_stored, 16)
            sp.wait_ge(out_stored, 16 * KT)

        @block.tensor
        def _(pe):
            def sum_squares(norm):
                for m in range(KT):
                    pe.wait_ge(squares_ready, number(norm * KT + m + 1))
                    pe.matmul(ps[:, 0, :], ones[:, :], square[:, m % 2, :],
                              start=(m == 0), stop=(m == KT - 1)).then_inc(squares_used, 1)

            def project(n, g, ks=range(KT), norm=None):
                if 0 in ks:
                    if above_zero(n.half):
                        pe.wait_ge(bank_read[n.slot], number(n.half))
                    pe.wait_ge(w_lo_ready, number(g + 1))
                for k in ks:
                    if norm is not None:
                        pe.wait_ge(u_lo_dve if k % 2 else u_lo_pool, number(norm * KT // 2 + k // 2 + 1))
                    blk = slice(k * P, (k + 1) * P)
                    out = ps[:, n.slot, :]
                    pe.matmul(out, w_hi[:, g.slot, blk], u_hi[:, k, :], start=(k == 0), stop=False)
                    pe.matmul(out, w_hi[:, g.slot, blk], u_lo[:, k, :], start=False, stop=False)
                    last = pe.matmul(out, w_lo[:, g.slot, blk], u_hi[:, k, :], start=False, stop=(k == KT - 1))
                if KT - 1 in ks:
                    last.then_inc(tile_done, 1)

            def turn_iw():
                pe.wait_ge(iwT_ready, 1)
                for i in range(1, QB):
                    last = pe.transpose(ps[:, T_BANK, (i - 1) * IDX_HEADS:i * IDX_HEADS],
                                        iwT[:, i * P:(i + 1) * P], ident[0:IDX_HEADS, 0:IDX_HEADS])
                last.then_inc(iw_turned, 1)

            def index_scores(t):
                pe.wait_ge(rope_lo_ready, number(t + (R_IQ + 1)))
                for s in range(2):
                    for kk, i in enumerate((3, 2, 1)):
                        if above_zero(t * 6 + (3 * s + kk - 5)):
                            pe.wait_ge(rel_ready, number(t * 6 + (3 * s + kk - 5)))
                        out = ps[:, (S_BANK, T_BANK)[s] + i - 1, 0:(i + 1) * P]
                        qs, ks = slice(i * P, (i + 1) * P), slice(0, (i + 1) * P)
                        pe.matmul(out, q_hi[:, t.slot, qs], ik[:, 2 * s, ks], start=True, stop=False)
                        pe.matmul(out, q_hi[:, t.slot, qs], ik[:, 2 * s + 1, ks], start=False, stop=False)
                        pe.matmul(out, q_lo[:, t.slot, qs], ik[:, 2 * s, ks], start=False,
                                  stop=True).then_inc(idx_done, 1)

            def turn_v(n):
                pe.wait_ge(bank_read[n.slot], number(n.half + 1))
                for j in range(QB):
                    last = pe.transpose(ps[:, T_BANK + 1, j * P:(j + 1) * P], v_f[:, j * P:(j + 1) * P], ident[:, :])
                last.then_inc(v_turned, 1)

            def scores(n, slot, r):
                pe.wait_ge(rope_lo_ready, number(r + 1))
                for kk, i in enumerate((3, 2, 1, 0)):
                    if above_zero(n * QB - QB + (1, 2, 4, 4)[kk]):
                        pe.wait_ge(scores_read, number(n * QB - QB + (1, 2, 4, 4)[kk]))
                    at = 2 * P if i == 0 else 0
                    out = ps[:, S_BANK + max(i, 1) - 1, at:at + (i + 1) * P]
                    qs, ks = slice(i * P, (i + 1) * P), slice(0, (i + 1) * P)
                    pe.matmul(out, q_hi[:, slot, qs], k_hi[:, ks], start=True, stop=False)
                    pe.matmul(out, q_hi[:, slot, qs], k_lo[:, ks], start=False, stop=False)
                    last = pe.matmul(out, q_lo[:, slot, qs], k_hi[:, ks], start=False, stop=True)
                    if i != 1:
                        last.then_inc(scores_done, 1)

            def turn_probs(n):
                pe.wait_ge(probs_ready, number(n * QB + QB))
                if above_zero(n):
                    pe.wait_ge(gated_ready, number(n))
                for b, js in enumerate(((0,), (1,), (2, 3))):
                    for j in js:
                        for i in range(j, QB):
                            at = T_OFF[j] - T_OFF[js[0]] + (i - j) * P
                            src = OFF[i] + j * P
                            last = pe.transpose(ps[:, T_BANK + b, at:at + P], probs[:, src:src + P], ident[:, :])
                    last.then_inc(probs_turned, 1)

            def output(n):
                for j in range(QB):
                    pe.wait_ge(pT_lo_ready, number(n * 3 + min(j, 2) + 1))
                    out = ps[:, T_BANK, j * P:SEQ]
                    vs, cols = slice(j * P, (j + 1) * P), slice(T_OFF[j], T_OFF[j] + SEQ - j * P)
                    pe.matmul(out, v_hi[:, vs], pT_hi[:, cols], start=(j == 0), stop=False)
                    pe.matmul(out, v_hi[:, vs], pT_lo[:, cols], start=False, stop=False)
                    last = pe.matmul(out, v_lo[:, vs], pT_hi[:, cols], start=False, stop=(j == QB - 1))
                last.then_inc(o_done, 1)

            def out_projection(layer, t, first=False, final=False):
                g = t + T_OUT[layer]
                pe.wait_ge(w_lo_ready, number(g + 1))
                pe.wait_ge(o_lo_ready, number(t + (layer * HEADS + 1)))
                for m in M_ORDER:
                    if first and m < 2:
                        pe.wait_ge(bank_read[m], number((PROJ_B + layer * 4 * HEADS + 1 - m) // 2))
                    if first and m == T_BANK:
                        pe.wait_ge(gated_ready, number((layer + 1) * HEADS))
                    blk = slice(m * P, (m + 1) * P)
                    pe.matmul(ps[:, m, :], w_hi[:, g.slot, blk], o_hi[:, t.slot, :], start=first, stop=False)
                    pe.matmul(ps[:, m, :], w_hi[:, g.slot, blk], o_lo[:, t.slot, :], start=False, stop=False)
                    last = pe.matmul(ps[:, m, :], w_lo[:, g.slot, blk], o_hi[:, t.slot, :], start=False, stop=final)
                    if m == M_ORDER[-1]:
                        last.then_inc(tile_done, 1)
                    elif final:
                        last.then_inc(y_done, 1)

            def out_projections(layer):
                out_projection(layer, Count(0), first=True)
                with pe.Fori(0, HEADS // 2 - 1) as i:
                    out_projection(layer, Count(1, 2, i))
                    out_projection(layer, Count(2, 2, i))
                out_projection(layer, Count(HEADS - 1), final=True)

            def head_a(h):
                attend, finish = (lo <= h.base < lo + HEADS or h.per for lo in (2, 3))
                query = h.base < HEADS + LATE_GATES or h.per
                if attend:
                    scores(h - 2, h.base % 2, h + (R_Q - 2))
                if query:
                    project(h + T_Q, h + T_Q, range(0, KT // 2))
                if finish:
                    output(h - 3)
                if query:
                    project(h + T_Q, h + T_Q, range(KT // 2, KT))
                if attend:
                    turn_probs(h - 2)

            def head_b(h):
                new, attend = h.base < HEADS or h.per, h.base > 0
                n, proj, tile = h + (HEADS - 1), h * 4 + PROJ_B, h * 4 + T_B
                if attend:
                    scores(n, 0, h * 2 + (R_B - 1))
                    project(proj - 1, tile - 1)
                if new:
                    project(proj, tile, norm=None if attend else 1)
                if attend:
                    turn_probs(n)
                if new:
                    project(proj + 1, tile + 1)
                    project(proj + 2, tile + 2)
                if attend:
                    output(n)
                if new:
                    turn_v(proj + 2)

            pe.wait_ge(ones_ready, 1)
            sum_squares(0)
            project(Count(T_IK), Count(T_IK), norm=0)
            project(Count(T_IQ), Count(T_IQ))
            pe.wait_ge(table_landed, 16 * 3)
            turn_iw()
            pe.wait_ge(iw_ready, 1)
            project(Count(T_IQ + 1), Count(T_IQ + 1))
            index_scores(Count(0))
            with pe.Fori(0, IDX_TILES // 2 - 1) as i:
                for j in range(2):
                    t = Count(2 + j, 2, i)
                    project(t + T_IQ, t + T_IQ)
                    index_scores(t - 1)
            index_scores(Count(IDX_TILES - 1))
            project(Count(T_V), Count(T_V))
            project(Count(T_K), Count(T_K))
            pe.wait_ge(rel_ready, 6 * IDX_TILES)
            turn_v(Count(T_V))
            project(Count(T_Z), Count(T_Z))
            with pe.Fori(0, EARLY_GATES // 2 - 1) as i:
                for j in range(2):
                    n = Count(T_Z + 1 + j, 2, i)
                    project(n, n)
            project(Count(T_Q - 1), Count(T_Q - 1))
            pe.wait_ge(v_lo_ready, 1)
            for h0 in range(3):
                head_a(Count(h0))
            with pe.Fori(0, HEADS // 2 - 2) as i:
                head_a(Count(3, 2, i))
                head_a(Count(4, 2, i))
            for h0 in range(HEADS - 1, HEADS + 3):
                head_a(Count(h0))
            out_projections(0)
            sum_squares(1)
            head_b(Count(0))
            with pe.Fori(0, HEADS - 1) as i:
                head_b(Count(1, 1, i))
            head_b(Count(HEADS))
            out_projections(1)
            sum_squares(2)

        @block.scalar
        def _(act):
            def split_w(g):
                act.wait_ge(w_landed[g.slot], number((g.half + 1) * 16))
                if above_zero(g - 1):
                    act.wait_ge(tile_done, number(g - 1))
                act.activation(w_hi[:, g.slot, :], w_raw[:, g.slot, :], ACT.Copy).then_inc(w_hi_ready, 1)

            def squares(norm):
                for at, m in enumerate(M_ORDER):
                    if norm == 0:
                        act.wait_ge(x_landed[m], 16)
                    else:
                        act.wait_ge(residual_ready, number((norm - 1) * KT + at + 1))
                    if above_zero(norm * KT + at - 1):
                        act.wait_ge(squares_used, number(norm * KT + at - 1))
                    act.activation(square[:, at % 2, :], h[:, m, :], ACT.Square).then_inc(squares_ready, 1)

            def root(norm):
                act.wait_ge(mean_ready, number(norm + 1))
                act.activation(rstd[:, :], rstd[:, :], ACT.Sqrt).then_inc(root_ready, 1)

            def split_u(norm):
                for k in range(KT):
                    act.wait_ge(u_ready, number(norm * KT + k + 1))
                    act.activation(u_hi[:, k, :], u_f[:, k % 4, :], ACT.Copy).then_inc(u_hi_ready, 1)

            def rope_hi(r, out):
                act.wait_ge(rotated_ready, number(r + 1))
                act.activation(out, rotated[:, r.slot, :], ACT.Copy).then_inc(rope_hi_ready, 1)

            def relu(t):
                for s in range(2):
                    for kk, i in enumerate((3, 2, 1)):
                        act.wait_ge(idx_done, number(t * 6 + (3 * s + kk + 1)))
                        if above_zero(t * 6 + (3 * s + kk - 5)):
                            act.wait_ge(score_ready, number(t * 6 + (3 * s + kk - 5)))
                        at = OFF[i] - P
                        act.activation(rel[s][:, at:at + (i + 1) * P],
                                       ps[:, (S_BANK, T_BANK)[s] + i - 1, 0:(i + 1) * P],
                                       ACT.Relu).then_inc(rel_ready, 1)

            def copy_v(n):
                act.wait_ge(tile_done, number(n[1] + 1))
                act.activation(v_f[:, :], ps[:, n[0].slot, :], ACT.Copy).then_inc(bank_read[n[0].slot], 1)

            def v_part(vn):
                act.wait_ge(v_turned, number(vn + 1))
                act.activation(v_hi[:, :], ps[:, T_BANK + 1, :], ACT.Copy).then_inc(v_hi_ready, 1)

            def silu(row, n, g):
                act.wait_ge(tile_done, number(g + 1))
                act.activation(gated[:, row.value, :], ps[:, n.slot, :], ACT.Silu).then_inc(bank_read[n.slot], 1)

            def exps(n):
                if above_zero(n * 3):
                    act.wait_ge(probs_turned, number(n * 3))
                for kk, i in enumerate((3, 2, 1, 0)):
                    act.wait_ge(scores_read, number(n * QB + (kk + 1)))
                    cols = slice(OFF[i], OFF[i] + (i + 1) * P)
                    act.activation(probs[:, cols], neg_s[:, cols], ACT.Exp, bias=neg_max[:, i:i + 1], scale=-1.0,
                                   accum_out=den[:, i:i + 1]).then_inc(exp_done, 1)

            def probs_hi(n):
                for b, (at, end) in enumerate(((0, T_OFF[1]), (T_OFF[1], T_OFF[2]), (T_OFF[2], COLS))):
                    act.wait_ge(probs_turned, number(n * 3 + (b + 1)))
                    act.activation(pT_hi[:, at:end], ps[:, T_BANK + b, 0:end - at],
                                   ACT.Copy).then_inc(pT_hi_ready, 1)

            def split_o(layer, t):
                act.wait_ge(gated_ready, number(t + (layer * HEADS + 1)))
                act.wait_ge(tile_done, number(t + (T_OUT[layer] - 1)))
                act.activation(o_hi[:, t.slot, :], gated[:, t.value, :], ACT.Copy).then_inc(o_hi_ready, 1)

            def head_a(h):
                attend, rope = (lo <= h.base < lo + HEADS or h.per for lo in (2, 1))
                if h.base < HEADS + LATE_GATES or h.per:
                    split_w(h + (T_Q + 1))
                if attend:
                    exps(h - 2)
                if rope:
                    rope_hi(h + (R_Q - 1), q_hi[:, (h.base - 1) % 2, :])
                if h.base > HEADS and not h.per:
                    silu(h - (LATE_GATES + 1), h + (T_Q - 1), h + (T_Q - 1))
                if attend:
                    probs_hi(h - 2)

            def head_b(h):
                new, attend = h.base < HEADS or h.per, h.base > 0
                n, proj, tile, r = h + (HEADS - 1), h * 4 + PROJ_B, h * 4 + T_B, h * 2 + R_B
                if attend:
                    split_w(tile)
                    exps(n)
                if new:
                    split_w(tile + 1)
                if attend:
                    silu(h - 1, proj - 1, tile - 1)
                    act.preload_act_table(ACT.Exp)
                if new:
                    split_w(tile + 2)
                if attend:
                    probs_hi(n)
                if new:
                    rope_hi(r, q_hi[:, 0, :])
                    split_w(tile + 3)
                    rope_hi(r + 1, k_hi[:, :])
                    copy_v((proj + 2, tile + 2))
                    v_part(h + 1)

            def out_projections(layer):
                def step(t):
                    if t.base < HEADS - 1 or t.per:
                        split_w(t + (T_OUT[layer] + 1))
                        split_o(layer, t + 1)
                    elif layer == 0:
                        split_w(t + (T_OUT[layer] + 1))

                step(Count(0))
                with act.Fori(0, HEADS // 2 - 1) as i:
                    step(Count(1, 2, i))
                    step(Count(2, 2, i))
                step(Count(HEADS - 1))

            act.dma_start(gain[:, :], gains).then_inc(gain_landed, 16)
            act.dma_start(table[:, 2:4, :], rope_tables[:, 2:4, :]).then_inc(table_landed, 16)
            act.dma_start(ident[:, :], ident_in).then_inc(table_landed, 16)
            act.dma_start(table[:, 0:2, :], rope_tables[:, 0:2, :]).then_inc(table_landed, 16)
            act.dma_start(bias_a[:, 0:P], causal_bias).then_inc(bias_landed, 16)
            act.dma_start(bias_b[:, :], dilated_bias).then_inc(bias_landed, 16)
            squares(0)
            split_w(Count(0))
            root(0)
            split_u(0)
            split_w(Count(1))
            act.wait_ge(tile_done, 1)
            act.activation(iwT[:, :], ps[32:32 + IDX_HEADS, 0, :], ACT.Copy, scale=IDX_SCALE).then_inc(iwT_ready, 1)
            act.wait_ge(ik_zeroed, 1)
            act.wait_ge(rotated_ready, 1)
            for s in range(2):
                for half in range(2):
                    to, of = slice(64 * half + 32 * s, 64 * half + 32 * s + 32), slice(64 * half, 64 * half + 32)
                    last = act.activation(ik[to, 2 * s, :], rotated[of, 0, :], ACT.Copy)
            last.then_inc(rope_hi_ready, 1)
            split_w(Count(T_IQ + 1))
            rope_hi(Count(R_IQ), q_hi[:, 0, :])

            def idx_step(t):
                split_w(t + (T_IQ + 1))
                relu(t - 1)
                rope_hi(t + R_IQ, q_hi[:, t.slot, :])

            idx_step(Count(1))
            act.preload_act_table(ACT.Silu)
            with act.Fori(0, IDX_TILES // 2 - 1) as i:
                idx_step(Count(2, 2, i))
                idx_step(Count(3, 2, i))
            relu(Count(IDX_TILES - 1))
            split_w(Count(T_K))
            copy_v((Count(T_V), Count(T_V)))
            split_w(Count(T_Z))
            act.wait_ge(score_ready, 6 * IDX_TILES)
            act.activation(left, score[:, :], ACT.Copy).then_inc(left_ready, 1)
            rope_hi(Count(R_K), k_hi[:, :])
            v_part(Count(0))

            def gate_step(z):
                n = z + T_Z
                split_w(n + 1)
                silu(z, n, n)

            gate_step(Count(0))
            with act.Fori(0, EARLY_GATES // 2 - 1) as i:
                gate_step(Count(1, 2, i))
                gate_step(Count(2, 2, i))
            gate_step(Count(EARLY_GATES - 1))
            act.preload_act_table(ACT.Exp)
            for h0 in range(3):
                head_a(Count(h0))
            with act.Fori(0, HEADS // 2 - 2) as i:
                head_a(Count(3, 2, i))
                head_a(Count(4, 2, i))
            for h0 in range(HEADS - 1, HEADS + 2):
                head_a(Count(h0))
            split_o(0, Count(0))
            head_a(Count(HEADS + 2))
            out_projections(0)
            squares(1)
            root(1)
            split_u(1)
            act.preload_act_table(ACT.Exp)
            head_b(Count(0))
            with act.Fori(0, HEADS - 1) as i:
                head_b(Count(1, 1, i))
            head_b(Count(HEADS))
            split_o(1, Count(0))
            out_projections(1)
            squares(2)
            root(2)

        @block.vector
        def _(dve):
            def norm(layer):
                if layer:
                    for at, m in enumerate(M_ORDER):
                        if at < KT - 1:
                            dve.wait_ge(y_done, number((layer - 1) * (KT - 1) + at + 1))
                        else:
                            dve.wait_ge(tile_done, number(T_OUT[layer - 1] + HEADS))
                        dve.tensor_tensor(h[:, m, :], ps[:, m, :], h[:, m, :], ALU.add).then_inc(residual_ready, 1)
                dve.wait_ge(squares_used, number((layer + 1) * KT))
                dve.tensor_scalar(rstd[:, :], ps[:, 0, :], 1.0 / D_MODEL, NORM_EPS, ALU.mult,
                                  ALU.add).then_inc(mean_ready, 1)
                dve.wait_ge(root_ready, number(layer + 1))
                dve.reciprocal(rstd[:, :], rstd[:, :]).then_inc(rstd_ready, 1)
                dve.wait_ge(rstd_ready, number(layer + 1))
                for k in range(KT):
                    out = h[:, k, :]
                    if layer < 2:
                        out = u_f[:, k % 4, :]
                        if k >= 4 and k % 2 == 0:
                            dve.wait_ge(u_lo_pool, number(layer * KT // 2 + (k - 4) // 2 + 1))
                    dve.scalar_tensor_tensor(out=out, in0=h[:, k, :], scalar=gain[:, layer * KT + k:layer * KT + k + 1],
                                             in1=rstd[:, :], op0=ALU.mult, op1=ALU.mult).then_inc(u_ready, 1)
                    if layer < 2 and k and k % 2 == 0:
                        u_part(layer, k - 1)
                if layer < 2:
                    u_part(layer, KT - 1)

            def u_part(layer, k):
                dve.wait_ge(u_hi_ready, number(layer * KT + k + 1))
                dve.tensor_tensor(u_lo[:, k, :], u_f[:, k % 4, :], u_hi[:, k, :].bitcast(F32),
                                  ALU.subtract).then_inc(u_lo_dve, 1)

            def rope(r, n, g, cos=0):
                dve.wait_ge(tile_done, number(g + 1))
                if above_zero(r):
                    dve.wait_ge(rotated_ready, number(r))
                raw, half = ps[:, n.slot, :], P // 2
                dve.tensor_tensor(by_sin[0:half, :], ps[half:P, n.slot, :], table[half:P, cos + 1, :], ALU.mult)
                dve.tensor_tensor(by_sin[half:P, :], ps[0:half, n.slot, :], table[0:half, cos + 1, :], ALU.mult)
                dve.tensor_tensor(by_cos[:, :], raw, table[:, cos, :], ALU.mult).then_inc(bank_read[n.slot], 1)
                dve.wait_ge(bank_read[n.slot], number(n.half + 1))
                if above_zero(r - 1):
                    dve.wait_ge(rope_lo_ready, number(r - 1))
                dve.tensor_tensor(rotated[:, r.slot, :], by_cos[:, :], by_sin[:, :],
                                  ALU.add).then_inc(rotated_ready, 1)

            def add_scores(t):
                for s in range(2):
                    for kk, i in enumerate((3, 2, 1)):
                        dve.wait_ge(rel_ready, number(t * 6 + (3 * s + kk + 1)))
                        if above_zero(t * 6 + (3 * s + kk - 2)):
                            dve.wait_ge(score_ready, number(t * 6 + (3 * s + kk - 2)))
                        cols = slice(OFF[i] - P, OFF[i] + i * P)
                        head = (t * 2 + s).value
                        dve.scalar_tensor_tensor(out=score[:, cols], in0=rel[s][:, cols],
                                                 scalar=iw[:, i - 1, bass.ds(head, 1)], in1=score[:, cols],
                                                 op0=ALU.mult, op1=ALU.add).then_inc(score_ready, 1)

            def take_eight(r):
                for i in range(1, QB):
                    if above_zero(r * 3 + (i - 3)):
                        least = in_register(dve, r * 3 + (i - 3))
                        dve.wait_ge(top8_taken, 1)
                        dve.wait_ge(top8_taken, least)
                    dve.max(top8[:, i - 1, :], left[:, OFF[i] - P:OFF[i] + i * P]).then_inc(top8_ready, 1)
                for i in range(1, QB):
                    least = in_register(dve, r * 3 + i)
                    dve.wait_ge(top8_ready, 1)
                    dve.wait_ge(top8_ready, least)
                    part = left[:, OFF[i] - P:OFF[i] + i * P]
                    dve.match_replace(part, top8[:, i - 1, :], part, NEG).then_inc(top8_taken, 1)

            def mask_scores(n, bias, offset):
                for kk, i in enumerate((3, 2, 1, 0)):
                    if i:
                        if above_zero(n * QB + (kk + 1 - QB)):
                            dve.wait_ge(exp_done, number(n * QB + (kk + 1 - QB)))
                        least = in_register(dve, n * 3 + (kk + 1))
                        dve.wait_ge(scores_done, 1)
                        dve.wait_ge(scores_done, least)
                    else:
                        if above_zero(n * QB):
                            least = in_register(dve, n * QB)
                            dve.wait_ge(exp_done, 1)
                            dve.wait_ge(exp_done, least)
                    at = 2 * P if i == 0 else 0
                    width = (i + 1) * P
                    dve.tensor_tensor_reduce(neg_s[:, OFF[i]:OFF[i] + width],
                                             ps[:, S_BANK + max(i, 1) - 1, at:at + width],
                                             bias[:, offset(i):offset(i) + width], -SCALE, -NEG, ALU.add, ALU.min,
                                             neg_max[:, i:i + 1]).then_inc(scores_read, 1)

            def invert(n):
                dve.wait_ge(exp_done, number(n * QB + QB))
                dve.reciprocal(inv_den[:, :], den[:, :]).then_inc(inv_ready, 1)

            def probs_lo(n):
                for b, (at, end) in enumerate(((0, T_OFF[1]), (T_OFF[1], T_OFF[2]), (T_OFF[2], COLS))):
                    dve.wait_ge(pT_hi_ready, number(n * 3 + (b + 1)))
                    dve.tensor_tensor(pT_lo[:, at:end], ps[:, T_BANK + b, 0:end - at],
                                      pT_hi[:, at:end].bitcast(F32), ALU.subtract).then_inc(pT_lo_ready, 1)

            def v_part(vn):
                dve.wait_ge(v_hi_ready, number(vn + 1))
                dve.tensor_tensor(v_lo[:, :], ps[:, T_BANK + 1, :], v_hi[:, :].bitcast(F32),
                                  ALU.subtract).then_inc(v_lo_ready, 1)

            def gate(n, row, z):
                dve.wait_ge(o_done, number(n + 1))
                dve.wait_ge(bank_read[z.slot], number(z.half + 1))
                dve.tensor_tensor(gated[:, row.value, :], ps[:, T_BANK, :], gated[:, row.value, :],
                                  ALU.mult).then_inc(gated_ready, 1)

            def head_a(h):
                attend, roped, finish = (lo <= h.base < lo + HEADS or h.per for lo in (2, 1, 3))
                if attend:
                    mask_scores(h - 2, bias_a, lambda i: OFF[i])
                if roped:
                    rope(h + (R_Q - 1), h + (T_Q - 1), h + (T_Q - 1))
                if attend:
                    invert(h - 2)
                if finish:
                    late = h.base - 3 >= EARLY_GATES and not h.per
                    gate(h - 3, h - 3, h + ((T_LATE - EARLY_GATES if late else T_Z) - 3))
                if attend:
                    probs_lo(h - 2)

            def head_b(h):
                new, attend = h.base < HEADS or h.per, h.base > 0
                n, proj, tile, r = h + (HEADS - 1), h * 4 + PROJ_B, h * 4 + T_B, h * 2 + R_B
                if attend:
                    mask_scores(n, bias_b, lambda i: SEQ - (i + 1) * P)
                    invert(n)
                if new:
                    rope(r, proj, tile)
                if attend:
                    probs_lo(n)
                if new:
                    rope(r + 1, proj + 1, tile + 1)
                if attend:
                    gate(n, h - 1, proj - 1)
                if new:
                    v_part(h + 1)

            dve.memset(ones[:, :], 1.0).then_inc(ones_ready, 1)
            dve.wait_ge(gain_landed, 16)
            norm(0)
            dve.wait_ge(table_landed, 16 * 3)
            dve.wait_ge(iwT_ready, 1)
            rope(Count(0), Count(0), Count(0), cos=2)
            dve.wait_ge(rope_hi_ready, 1)
            for s in range(2):
                for half in range(2):
                    to, of = slice(64 * half + 32 * s, 64 * half + 32 * s + 32), slice(64 * half, 64 * half + 32)
                    last = dve.tensor_tensor(ik[to, 2 * s + 1, :], rotated[of, 0, :], ik[of, 0, :].bitcast(F32),
                                             ALU.subtract)
            last.then_inc(rope_lo_ready, 1)
            rope(Count(R_IQ), Count(T_IQ), Count(T_IQ), cos=2)
            dve.wait_ge(iw_turned, 1)
            dve.tensor_copy(iw[:, :, :], ps[:, T_BANK, 0:(QB - 1) * IDX_HEADS].rearrange(
                "p (i n) -> p i n", n=IDX_HEADS)).then_inc(iw_ready, 1)
            dve.wait_ge(iw_ready, 1)
            dve.wait_ge(score_zeroed, 2)
            rope(Count(R_IQ + 1), Count(T_IQ + 1), Count(T_IQ + 1), cos=2)
            add_scores(Count(0))
            with dve.Fori(0, IDX_TILES // 2 - 1) as i:
                for j in range(2):
                    t = Count(2 + j, 2, i)
                    rope(t + R_IQ, t + T_IQ, t + T_IQ, cos=2)
                    add_scores(t - 1)
            add_scores(Count(IDX_TILES - 1))
            rope(Count(R_K), Count(T_K), Count(T_K))
            v_part(Count(0))
            dve.wait_ge(left_ready, 1)
            take_eight(Count(0))
            with dve.Fori(0, TOP_K // 8 - 1) as i:
                take_eight(Count(1, 1, i))
            dve.wait_ge(top8_taken, 3 * TOP_K // 8)
            dve.tensor_tensor(bias_a[:, P:COLS], score[:, :], left, ALU.is_gt).then_inc(chosen_ready, 1)
            dve.wait_ge(chosen_ready, 1)
            dve.tensor_scalar(bias_a[:, P:COLS], bias_a[:, P:COLS], -1.0, -NEG, ALU.add,
                              ALU.mult).then_inc(bias_ready, 1)
            dve.wait_ge(bias_ready, 1)
            dve.wait_ge(bias_landed, 32)
            for h0 in range(3):
                head_a(Count(h0))
            with dve.Fori(0, HEADS // 2 - 2) as i:
                head_a(Count(3, 2, i))
                head_a(Count(4, 2, i))
            for h0 in range(HEADS - 1, HEADS + 3):
                head_a(Count(h0))
            norm(1)
            head_b(Count(0))
            with dve.Fori(0, HEADS - 1) as i:
                head_b(Count(1, 1, i))
            head_b(Count(HEADS))
            norm(2)

        @block.gpsimd
        def _(pool):
            def split_w(g):
                pool.wait_ge(w_hi_ready, number(g + 1))
                pool.tensor_tensor(w_lo[:, g.slot, :], w_raw[:, g.slot, :], w_hi[:, g.slot, :].bitcast(F32),
                                   ALU.subtract).then_inc(w_lo_ready, 1)

            def split_u(norm):
                for k in range(0, KT, 2):
                    pool.wait_ge(u_hi_ready, number(norm * KT + k + 1))
                    pool.tensor_tensor(u_lo[:, k, :], u_f[:, k % 4, :], u_hi[:, k, :].bitcast(F32),
                                       ALU.subtract).then_inc(u_lo_pool, 1)

            def rope_lo(r, hi, lo):
                pool.wait_ge(rope_hi_ready, number(r + 1))
                pool.tensor_tensor(lo, rotated[:, r.slot, :], hi.bitcast(F32), ALU.subtract).then_inc(rope_lo_ready, 1)

            def normalise(n):
                least = in_register(pool, n + 1)
                pool.wait_ge(inv_ready, 1)
                pool.wait_ge(inv_ready, least)
                for i in (3, 2, 1, 0):
                    cols = slice(OFF[i], OFF[i] + (i + 1) * P)
                    pool.tensor_scalar(probs[:, cols], probs[:, cols], inv_den[:, i:i + 1], 1.0, ALU.mult,
                                       ALU.mult).then_inc(probs_ready, 1)

            def split_o(layer, t):
                pool.wait_ge(o_hi_ready, number(t + (layer * HEADS + 1)))
                pool.tensor_tensor(o_lo[:, t.slot, :], gated[:, t.value, :], o_hi[:, t.slot, :].bitcast(F32),
                                   ALU.subtract).then_inc(o_lo_ready, 1)

            def head_a(h):
                attend, rope = (lo <= h.base < lo + HEADS or h.per for lo in (2, 1))
                if h.base < HEADS + LATE_GATES or h.per:
                    split_w(h + (T_Q + 1))
                if attend:
                    normalise(h - 2)
                if rope:
                    slot = (h.base - 1) % 2
                    rope_lo(h + (R_Q - 1), q_hi[:, slot, :], q_lo[:, slot, :])

            def head_b(h):
                new, attend = h.base < HEADS or h.per, h.base > 0
                tile, r = h * 4 + T_B, h * 2 + R_B
                if attend:
                    split_w(tile)
                    normalise(h + (HEADS - 1))
                if new:
                    split_w(tile + 1)
                    split_w(tile + 2)
                    rope_lo(r, q_hi[:, 0, :], q_lo[:, 0, :])
                    split_w(tile + 3)
                    rope_lo(r + 1, k_hi[:, :], k_lo[:, :])

            def out_projections(layer):
                def step(t):
                    if t.base < HEADS - 1 or t.per:
                        split_w(t + (T_OUT[layer] + 1))
                        split_o(layer, t + 1)
                    elif layer == 0:
                        split_w(t + (T_OUT[layer] + 1))

                step(Count(0))
                with pool.Fori(0, HEADS // 2 - 1) as i:
                    step(Count(1, 2, i))
                    step(Count(2, 2, i))
                step(Count(HEADS - 1))

            pool.memset(ik[:, :, :].bitcast(F32), 0.0).then_inc(ik_zeroed, 1)
            pool.memset(score[:, :], 0.0).then_inc(score_zeroed, 1)
            split_w(Count(0))
            split_u(0)
            split_w(Count(1))
            pool.wait_ge(score_zeroed, 1)
            pool.wait_ge(bias_landed, 32)
            for i in range(1, QB):
                last = pool.tensor_copy(score[:, OFF[i] - P + i * P:OFF[i] + i * P], bias_a[:, 0:P])
            last.then_inc(score_zeroed, 1)

            def idx_step(t):
                split_w(t + (T_IQ + 1))
                rope_lo(t + R_IQ, q_hi[:, t.slot, :], q_lo[:, t.slot, :])

            idx_step(Count(0))
            idx_step(Count(1))
            with pool.Fori(0, IDX_TILES // 2 - 1) as i:
                idx_step(Count(2, 2, i))
                idx_step(Count(3, 2, i))
            split_w(Count(T_K))
            split_w(Count(T_Z))
            rope_lo(Count(R_K), k_hi[:, :], k_lo[:, :])
            split_w(Count(T_Z + 1))
            with pool.Fori(0, EARLY_GATES // 2 - 1) as i:
                split_w(Count(T_Z + 2, 2, i))
                split_w(Count(T_Z + 3, 2, i))
            split_w(Count(T_Q))
            for h0 in range(3):
                head_a(Count(h0))
            with pool.Fori(0, HEADS // 2 - 2) as i:
                head_a(Count(3, 2, i))
                head_a(Count(4, 2, i))
            for h0 in range(HEADS - 1, HEADS + 3):
                head_a(Count(h0))
            split_o(0, Count(0))
            out_projections(0)
            split_u(1)
            head_b(Count(0))
            with pool.Fori(0, HEADS - 1) as i:
                head_b(Count(1, 1, i))
            head_b(Count(HEADS))
            split_o(1, Count(0))
            out_projections(1)


def rotary_table(rows_per_head, sin):
    dim = 2 * rows_per_head
    freqs = np.float32(10000.0) ** (-np.arange(0, dim, 2, dtype=np.float32) / np.float32(dim))
    angle = np.arange(SEQ, dtype=np.float32)[None, :] * freqs[np.arange(P) % rows_per_head][:, None]
    if not sin:
        return np.cos(angle)
    return np.sin(angle) * np.where(np.arange(P) < P // 2, 1, -1).astype(np.float32)[:, None]


def constants():
    dist = np.arange(P)[:, None] - (np.arange(SEQ)[None, :] - (SEQ - P))
    times = sum(((dist >= 0) & (dist <= window) & (dist % dilation == 0)).astype(np.float64)
                for window, dilation in CONFIGS)
    dilated = np.where(times > 0, np.log(np.maximum(times, 1)) / SCALE, NEG).astype(np.float32)
    causal = np.where(np.arange(P)[:, None] >= np.arange(P)[None, :], 0, NEG).astype(np.float32)
    tables = np.stack([rotary_table(64, False), rotary_table(64, True), rotary_table(32, False),
                       rotary_table(32, True)], 1)
    return tables.astype(np.float32), dilated, causal, np.eye(P, dtype=np.float32)


def tiles_of(w):
    n = w.shape[1] // P
    return w.reshape(KT, P, n, P).transpose(2, 1, 0, 3).reshape(n, P, D_MODEL)


def kernel(**inputs):
    from concourse import bacc
    from concourse.bass_utils import run_bass_kernel_spmd

    a_in, b_in = np.asarray(inputs["a_w_in"])[0], np.asarray(inputs["b_w_in"])[0]
    ends = np.cumsum([D_INNER, HEAD_DIM, HEAD_DIM, IDX_HEADS * IDX_DIM, IDX_DIM, IDX_HEADS])
    aq, ak, av, aiq, aik, aiw, az = np.split(a_in, ends, axis=1)
    half = IDX_DIM // 2
    first = np.zeros((D_MODEL, P), a_in.dtype)
    first[:, 0:half], first[:, 64:64 + half] = aik[:, :half], aik[:, half:]
    first[:, half:half + IDX_HEADS] = aiw
    aiq = aiq.reshape(D_MODEL, IDX_TILES, 2, 2, half).transpose(0, 1, 3, 2, 4).reshape(D_MODEL, IDX_HEADS * IDX_DIM)
    b_in = b_in.reshape(D_MODEL, 4, HEADS, HEAD_DIM).transpose(0, 2, 1, 3).reshape(D_MODEL, 4 * D_INNER)
    weights = np.concatenate(
        [tiles_of(first), tiles_of(aiq), tiles_of(av), tiles_of(ak), tiles_of(az)[:EARLY_GATES], tiles_of(aq),
         tiles_of(az)[EARLY_GATES:], np.asarray(inputs["a_w_out"])[0].reshape(HEADS, P, D_MODEL), tiles_of(b_in),
         np.asarray(inputs["b_w_out"])[0].reshape(HEADS, P, D_MODEL)])
    gains = np.concatenate([np.asarray(inputs["norm_g"]), np.asarray(inputs["final_g"])[None]])
    gains = gains.reshape(3, KT, P).transpose(2, 0, 1).reshape(P, 3 * KT)
    tables, dilated, causal, ident = constants()
    arrays = {
        "x_turned": np.asarray(inputs["x"])[0].T, "gains": gains, "weights": weights, "rope_tables": tables,
        "dilated_bias": dilated, "causal_bias": causal, "identity": ident,
    }
    arrays = {name: np.ascontiguousarray(a) for name, a in arrays.items()}
    nc = bacc.Bacc("TRN2", target_bir_lowering=False, num_devices=1)
    args = [nc.dram_tensor(name, a.shape, mybir.dt.from_np(a.dtype), kind="ExternalInput").ap()
            for name, a in arrays.items()]
    args.append(nc.dram_tensor("outT", (D_MODEL, SEQ), F32, kind="ExternalOutput").ap())
    build(nc, *args)
    r = run_bass_kernel_spmd(nc, [arrays], core_ids=[0])
    return np.asarray(r.results[0]["outT"]).T.reshape(1, SEQ, D_MODEL)
```

```python
from contextlib import ExitStack

import numpy as np

import concourse.bass as bass
from concourse import mybir

F32 = mybir.dt.float32
F32R = mybir.dt.float32r
ALU = mybir.AluOpType
ACT = mybir.ActivationFunctionType

P = 128
D_MODEL, SEQ, D_INNER = 1024, 512, 2048
KT = D_MODEL // P
QB = SEQ // P
HEADS, HEAD_DIM = 16, 128
IDX_HEADS, IDX_DIM = 16, 64
IDX_TILES = IDX_HEADS * IDX_DIM // P
TOP_K = min(256, SEQ // 4)
NORM_EPS = 1e-6
SCALE = HEAD_DIM ** -0.5
IDX_SCALE = IDX_HEADS ** -0.5 * IDX_DIM ** -0.5
NEG = -3e38
CONFIGS = ((128, 1), (512, 4), (2048, 16))

OFF = [P * i * (i + 1) // 2 for i in range(QB)]
COLS = P * QB * (QB + 1) // 2
T_OFF = [0, SEQ, SEQ + 3 * P, SEQ + 5 * P]

T_IK, T_IQ, T_V, T_K, T_Z = 0, 1, 1 + IDX_TILES, 2 + IDX_TILES, 3 + IDX_TILES
LATE_GATES = 2
EARLY_GATES = HEADS - LATE_GATES
T_Q = T_Z + EARLY_GATES
T_LATE = T_Q + HEADS
T_OUT = [T_LATE + LATE_GATES, T_LATE + LATE_GATES + HEADS + 4 * HEADS]
T_B = T_OUT[0] + HEADS
TILES = T_OUT[1] + HEADS
PROJ_B = T_OUT[0]
R_IQ, R_K = 1, 1 + IDX_TILES
R_Q = R_K + 1
R_B = R_Q + HEADS
assert TOP_K == P == 8 * HEADS and T_OFF[-1] + P == COLS

M_ORDER = (0, 1, 2, 3, 4, 6, 7, 5)
POOL_OUT = (2, 5)
SQUARES = 3
S_BANK, T_BANK = 2, 5


class Count:

    def __init__(self, base, per=0, turn=None):
        self.base, self.per, self.turn = base, per, turn

    def __add__(self, k):
        return Count(self.base + k, self.per, self.turn)

    def __sub__(self, k):
        return self + (-k)

    def __mul__(self, k):
        return Count(self.base * k, self.per * k, self.turn)

    @property
    def value(self):
        return self.turn * self.per + self.base if self.per else self.base

    @property
    def slot(self):
        assert self.per % 2 == 0
        return self.base % 2

    @property
    def half(self):
        assert self.per % 2 == 0
        return Count(self.base // 2, self.per // 2, self.turn)


def number(count):
    return count.value if isinstance(count, Count) else count


def above_zero(count):
    return (count.base if isinstance(count, Count) else count) > 0


def in_register(eng, count):
    return eng.to_reg(count.value) if count.per else count.base


def build(nc, xT, gains, weights, rope_tables, dilated_bias, causal_bias, ident_in, outT):
    with ExitStack() as ctx:
        def sb(name, shape, dt=F32):
            return ctx.enter_context(nc.sbuf_tensor(name, shape, dt))

        def sem(name):
            return ctx.enter_context(nc.semaphore(name))

        ps = ctx.enter_context(nc.psum_tensor("ps", [P, 8, SEQ], F32))

        w_raw = sb("w_raw", [P, 2, D_MODEL])
        w_hi = sb("w_hi", [P, 2, D_MODEL], F32R)
        w_lo = sb("w_lo", [P, 2, D_MODEL], F32R)
        h = sb("h", [P, KT, SEQ])
        u_hi = sb("u_hi", [P, KT, SEQ], F32R)
        u_lo = sb("u_lo", [P, KT, SEQ], F32R)
        gain = sb("gain", [P, 3 * KT])
        square = sb("square", [P, SQUARES, SEQ])
        square_sum = sb("square_sum", [P, SEQ])
        rstd = sb("rstd", [P, SEQ])
        root_turned = sb("root_turned", [P, QB])
        inv_turned = sb("inv_turned", [P, QB])
        eps = sb("eps", [P, 1])
        ones = sb("ones", [P, P])
        ident = sb("ident", [P, P])
        table = sb("table", [P, 4, SEQ])
        scaled = sb("scaled", [P, 2, SEQ])
        by_cos = sb("by_cos", [P, SEQ])
        by_sin = sb("by_sin", [P, SEQ])
        rotated = sb("rotated", [P, 2, SEQ])
        q_hi = sb("q_hi", [P, 2, SEQ], F32R)
        q_lo = sb("q_lo", [P, 2, SEQ], F32R)
        k_hi = sb("k_hi", [P, SEQ], F32R)
        k_lo = sb("k_lo", [P, SEQ], F32R)
        v_f = sb("v_f", [P, SEQ])
        v_hi = sb("v_hi", [P, SEQ], F32R)
        v_lo = sb("v_lo", [P, SEQ], F32R)
        bias_a = sb("bias_a", [P, COLS])
        bias_b = sb("bias_b", [P, SEQ])
        neg_s = sb("neg_s", [P, COLS])
        neg_max = sb("neg_max", [P, QB])
        probs = sb("probs", [P, COLS])
        den = sb("den", [P, QB])
        inv_den = sb("inv_den", [P, QB])
        pT_hi = sb("pT_hi", [P, COLS], F32R)
        pT_lo = sb("pT_lo", [P, COLS], F32R)
        z_f = sb("z_f", [P, SEQ])
        gated = sb("gated", [P, HEADS, SEQ])
        o_hi = sb("o_hi", [P, 2, SEQ], F32R)
        o_lo = sb("o_lo", [P, 2, SEQ], F32R)
        ik = sb("ik", [P, 4, SEQ], F32R)
        iwT = sb("iwT", [IDX_HEADS, SEQ])
        iw = sb("iw", [P, QB - 1, IDX_HEADS])
        rel = [neg_s[:, 0:COLS - P], probs[:, 0:COLS - P]]
        score = sb("score", [P, COLS - P])
        left = rel[0]
        top8 = sb("top8", [P, QB - 1, 8])

        x_landed = [sem(f"x_landed{m}") for m in range(KT)]
        gain_landed, table_landed, bias_landed = sem("gain_landed"), sem("table_landed"), sem("bias_landed")
        w_landed = [sem("w_landed0"), sem("w_landed1")]
        w_hi_ready, w_lo_ready, tile_done = sem("w_hi_ready"), sem("w_lo_ready"), sem("tile_done")
        ones_ready, squares_ready, squares_added = sem("ones_ready"), sem("squares_ready"), sem("squares_added")
        squares_used, sum_done, root_ready, rstd_ready = (
            sem("squares_used"), sem("sum_done"), sem("root_ready"), sem("rstd_ready"))
        idx_scaled, tables_scaled = sem("idx_scaled"), sem("tables_scaled")
        u_hi_ready, u_lo_ready = sem("u_hi_ready"), sem("u_lo_ready")
        iwT_raw, first_ready = sem("iwT_raw"), sem("first_ready")
        inv_turned_ready, diagonal_ready, spread_done = (
            sem("inv_turned_ready"), sem("diagonal_ready"), sem("spread_done"))
        silu_ready, eps_ready = sem("silu_ready"), sem("eps_ready")
        out_dve, out_half, out_pool = sem("out_dve"), sem("out_half"), sem("out_pool")
        bank_read = [sem("bank_read0"), sem("bank_read1")]
        rotated_ready = sem("rotated_ready")
        rope_hi_ready, rope_lo_ready = sem("rope_hi_ready"), sem("rope_lo_ready")
        ik_zeroed, iwT_ready, iw_turned, iw_ready = (
            sem("ik_zeroed"), sem("iwT_ready"), sem("iw_turned"), sem("iw_ready"))
        idx_done, rel_ready, score_ready = sem("idx_done"), sem("rel_ready"), sem("score_ready")
        score_zeroed, left_ready, top8_ready, top8_taken = (
            sem("score_zeroed"), sem("left_ready"), sem("top8_ready"), sem("top8_taken"))
        chosen_ready, bias_ready = sem("chosen_ready"), sem("bias_ready")
        v_turned, v_hi_ready, v_lo_ready = sem("v_turned"), sem("v_hi_ready"), sem("v_lo_ready")
        scores_done, scores_read, exp_done, inv_ready, probs_ready = (
            sem("scores_done"), sem("scores_read"), sem("exp_done"), sem("inv_ready"), sem("probs_ready"))
        probs_turned, pT_hi_ready, pT_lo_ready, o_done, gated_ready = (
            sem("probs_turned"), sem("pT_hi_ready"), sem("pT_lo_ready"), sem("o_done"), sem("gated_ready"))
        o_lo_ready, o_hi_ready, y_done, residual_ready = (
            sem("o_lo_ready"), sem("o_hi_ready"), sem("y_done"), sem("residual_ready"))
        out_stored = sem("out_stored")

        block = ctx.enter_context(nc.Block())

        @block.sync
        def _(sp):
            def load_tile(g):
                if above_zero(g - 1):
                    sp.wait_ge(w_lo_ready, number(g - 1))
                sp.dma_start(w_raw[:, g.slot, :], weights[g.value]).then_inc(w_landed[g.slot], 16)

            load_tile(Count(0))
            for m in M_ORDER:
                sp.dma_start(h[:, m, :], xT[m * P:(m + 1) * P, :]).then_inc(x_landed[m], 16)
            load_tile(Count(1))
            sp.dma_start(ident[:, :], ident_in).then_inc(table_landed, 16)
            sp.dma_start(table[:, 2:4, :], rope_tables[:, 2:4, :]).then_inc(table_landed, 16)
            sp.dma_start(table[:, 0:2, :], rope_tables[:, 0:2, :]).then_inc(table_landed, 16)
            sp.dma_start(bias_a[:, 0:P], causal_bias).then_inc(bias_landed, 16)
            sp.dma_start(bias_b[:, :], dilated_bias).then_inc(bias_landed, 16)
            with sp.Fori(0, TILES // 2 - 1) as i:
                load_tile(Count(2, 2, i))
                load_tile(Count(3, 2, i))
            for g in range(TILES // 2 * 2, TILES):
                load_tile(Count(g))
            for at, m in enumerate(M_ORDER):
                if at in POOL_OUT:
                    sp.wait_ge(out_pool, POOL_OUT.index(at) + 1)
                else:
                    sp.wait_ge(out_dve, at + 1 - sum(p < at for p in POOL_OUT))
                sp.dma_start(outT[m * P:(m + 1) * P, :], h[:, m, :]).then_inc(out_stored, 16)
            sp.wait_ge(out_stored, 16 * KT)

        @block.tensor
        def _(pe):
            def sum_squares(layer):
                pe.wait_ge(squares_added, number((layer + 1) * (KT - 1)))
                pe.matmul(ps[:, S_BANK, :], ones[:, :], square_sum[:, :], start=True, stop=True).then_inc(sum_done, 1)

            def sum_last_squares():
                for at in range(KT):
                    pe.wait_ge(squares_ready, number(2 * KT + at + 1))
                    for i in range(QB):
                        last = pe.matmul(ps[:, 0, i:i + 1], square[:, at % SQUARES, i * P:(i + 1) * P], ones[:, 0:1],
                                         start=(at == 0 and i == 0), stop=(at == KT - 1 and i == QB - 1))
                    if at < KT - 1:
                        last.then_inc(squares_used, 1)
                    else:
                        last.then_inc(sum_done, 1)
                pe.wait_ge(diagonal_ready, QB)
                pe.matmul(ps[:, 1, :], ones[:, :], square_sum[:, :], start=True, stop=True).then_inc(spread_done, 1)

            def project(n, g, part=range(KT), layer=None):
                if 0 in part:
                    if above_zero(n.half):
                        pe.wait_ge(bank_read[n.slot], number(n.half))
                    pe.wait_ge(w_lo_ready, number(g + 1))
                for at in part:
                    k = M_ORDER[at]
                    if layer is not None:
                        pe.wait_ge(u_lo_ready, number(layer * KT + at + 1))
                    blk = slice(k * P, (k + 1) * P)
                    out = ps[:, n.slot, :]
                    pe.matmul(out, w_hi[:, g.slot, blk], u_hi[:, k, :], start=(at == 0), stop=False)
                    pe.matmul(out, w_hi[:, g.slot, blk], u_lo[:, k, :], start=False, stop=False)
                    last = pe.matmul(out, w_lo[:, g.slot, blk], u_hi[:, k, :], start=False, stop=(at == KT - 1))
                if KT - 1 in part:
                    last.then_inc(tile_done, 1)

            def second_project(layer, n, g, first):
                project(n, g, range(0, first))
                sum_squares(layer)
                project(n, g, range(first, KT))

            def turn_iw():
                pe.wait_ge(iwT_ready, 1)
                for i in range(1, QB):
                    last = pe.transpose(ps[:, T_BANK, (i - 1) * IDX_HEADS:i * IDX_HEADS],
                                        iwT[:, i * P:(i + 1) * P], ident[0:IDX_HEADS, 0:IDX_HEADS])
                last.then_inc(iw_turned, 1)

            def index_scores(t):
                pe.wait_ge(rope_lo_ready, number(t + (R_IQ + 1)))
                for s in range(2):
                    for kk, i in enumerate((3, 2, 1)):
                        if above_zero(t * 6 + (3 * s + kk - 5)):
                            pe.wait_ge(rel_ready, number(t * 6 + (3 * s + kk - 5)))
                        out = ps[:, (S_BANK, T_BANK)[s] + i - 1, 0:(i + 1) * P]
                        qs, ks = slice(i * P, (i + 1) * P), slice(0, (i + 1) * P)
                        pe.matmul(out, q_hi[:, t.slot, qs], ik[:, 2 * s, ks], start=True, stop=False)
                        pe.matmul(out, q_hi[:, t.slot, qs], ik[:, 2 * s + 1, ks], start=False, stop=False)
                        pe.matmul(out, q_lo[:, t.slot, qs], ik[:, 2 * s, ks], start=False,
                                  stop=True).then_inc(idx_done, 1)

            def turn_v(n):
                pe.wait_ge(bank_read[n.slot], number(n.half + 1))
                for j in range(QB):
                    last = pe.transpose(ps[:, T_BANK + 1, j * P:(j + 1) * P], v_f[:, j * P:(j + 1) * P], ident[:, :])
                last.then_inc(v_turned, 1)

            def scores(n, slot, r):
                pe.wait_ge(rope_lo_ready, number(r + 1))
                for kk, i in enumerate((3, 2, 1, 0)):
                    if above_zero(n * QB - QB + (1, 2, 4, 4)[kk]):
                        pe.wait_ge(scores_read, number(n * QB - QB + (1, 2, 4, 4)[kk]))
                    at = 2 * P if i == 0 else 0
                    out = ps[:, S_BANK + max(i, 1) - 1, at:at + (i + 1) * P]
                    qs, ks = slice(i * P, (i + 1) * P), slice(0, (i + 1) * P)
                    pe.matmul(out, q_hi[:, slot, qs], k_hi[:, ks], start=True, stop=False)
                    pe.matmul(out, q_hi[:, slot, qs], k_lo[:, ks], start=False, stop=False)
                    last = pe.matmul(out, q_lo[:, slot, qs], k_hi[:, ks], start=False, stop=True)
                    if i != 1:
                        last.then_inc(scores_done, 1)

            def turn_probs(n):
                pe.wait_ge(probs_ready, number(n * QB + QB))
                if above_zero(n):
                    pe.wait_ge(gated_ready, number(n))
                for b, js in enumerate(((0,), (1,), (2, 3))):
                    for j in js:
                        for i in range(j, QB):
                            at = T_OFF[j] - T_OFF[js[0]] + (i - j) * P
                            src = OFF[i] + j * P
                            last = pe.transpose(ps[:, T_BANK + b, at:at + P], probs[:, src:src + P], ident[:, :])
                    last.then_inc(probs_turned, 1)

            def output(n):
                for j in range(QB):
                    pe.wait_ge(pT_lo_ready, number(n * 3 + min(j, 2) + 1))
                    out = ps[:, T_BANK, j * P:SEQ]
                    vs, cols = slice(j * P, (j + 1) * P), slice(T_OFF[j], T_OFF[j] + SEQ - j * P)
                    pe.matmul(out, v_hi[:, vs], pT_hi[:, cols], start=(j == 0), stop=False)
                    pe.matmul(out, v_hi[:, vs], pT_lo[:, cols], start=False, stop=False)
                    last = pe.matmul(out, v_lo[:, vs], pT_hi[:, cols], start=False, stop=(j == QB - 1))
                last.then_inc(o_done, 1)

            def out_projection(layer, t, first=False, final=False):
                g = t + T_OUT[layer]
                pe.wait_ge(w_lo_ready, number(g + 1))
                pe.wait_ge(o_lo_ready, number(t + (layer * HEADS + 1)))
                for m in M_ORDER:
                    if first and m < 2:
                        pe.wait_ge(bank_read[m], number((PROJ_B + layer * 4 * HEADS + 1 - m) // 2))
                    if first and m == T_BANK:
                        pe.wait_ge(gated_ready, number((layer + 1) * HEADS))
                    blk = slice(m * P, (m + 1) * P)
                    pe.matmul(ps[:, m, :], w_hi[:, g.slot, blk], o_hi[:, t.slot, :], start=first, stop=False)
                    pe.matmul(ps[:, m, :], w_hi[:, g.slot, blk], o_lo[:, t.slot, :], start=False, stop=False)
                    last = pe.matmul(ps[:, m, :], w_lo[:, g.slot, blk], o_hi[:, t.slot, :], start=False, stop=final)
                    if m == M_ORDER[-1]:
                        last.then_inc(tile_done, 1)
                    elif final:
                        last.then_inc(y_done, 1)

            def out_projections(layer):
                out_projection(layer, Count(0), first=True)
                with pe.Fori(0, HEADS // 2 - 1) as i:
                    out_projection(layer, Count(1, 2, i))
                    out_projection(layer, Count(2, 2, i))
                out_projection(layer, Count(HEADS - 1), final=True)

            def head_a(h):
                attend, finish = (lo <= h.base < lo + HEADS or h.per for lo in (2, 3))
                query = h.base < HEADS + LATE_GATES or h.per
                if attend:
                    scores(h - 2, h.base % 2, h + (R_Q - 2))
                if query:
                    project(h + T_Q, h + T_Q, range(0, KT // 2))
                if finish:
                    output(h - 3)
                if query:
                    project(h + T_Q, h + T_Q, range(KT // 2, KT))
                if attend:
                    turn_probs(h - 2)

            def head_b(h):
                new, attend = h.base < HEADS or h.per, h.base > 0
                n, proj, tile = h + (HEADS - 1), h * 4 + PROJ_B, h * 4 + T_B
                if attend:
                    scores(n, 0, h * 2 + (R_B - 1))
                    project(proj - 1, tile - 1)
                if new:
                    project(proj, tile, layer=None if attend else 1)
                if attend:
                    turn_probs(n)
                if attend and new:
                    project(proj + 1, tile + 1)
                elif new:
                    second_project(1, proj + 1, tile + 1, 2)
                if new:
                    project(proj + 2, tile + 2)
                if attend:
                    output(n)
                if new:
                    turn_v(proj + 2)

            pe.wait_ge(ones_ready, 1)
            project(Count(T_IK), Count(T_IK), layer=0)
            second_project(0, Count(T_IQ), Count(T_IQ), 1)
            second = Count(T_IQ + 1)
            project(second, second, range(0, KT // 2))
            pe.wait_ge(table_landed, 16 * 3)
            turn_iw()
            project(second, second, range(KT // 2, KT))
            pe.wait_ge(iw_ready, 1)
            def idx_step(t):
                project(t + T_IQ, t + T_IQ, range(0, KT // 2))
                index_scores(t - 2)
                project(t + T_IQ, t + T_IQ, range(KT // 2, KT))

            idx_step(Count(2))
            with pe.Fori(0, IDX_TILES // 2 - 1) as i:
                idx_step(Count(3, 2, i))
                idx_step(Count(4, 2, i))
            idx_step(Count(IDX_TILES + 1))
            project(Count(T_Z), Count(T_Z))
            pe.wait_ge(rel_ready, 6 * IDX_TILES)
            turn_v(Count(T_V))
            with pe.Fori(0, EARLY_GATES // 2 - 1) as i:
                for j in range(2):
                    n = Count(T_Z + 1 + j, 2, i)
                    project(n, n)
            project(Count(T_Q - 1), Count(T_Q - 1))
            pe.wait_ge(v_lo_ready, 1)
            for h0 in range(3):
                head_a(Count(h0))
            with pe.Fori(0, HEADS // 2 - 2) as i:
                head_a(Count(3, 2, i))
                head_a(Count(4, 2, i))
            for h0 in range(HEADS - 1, HEADS + 3):
                head_a(Count(h0))
            out_projections(0)
            pe.wait_ge(residual_ready, M_ORDER.index(PROJ_B % 2) + 1)
            head_b(Count(0))
            with pe.Fori(0, HEADS - 1) as i:
                head_b(Count(1, 1, i))
            head_b(Count(HEADS))
            out_projections(1)
            sum_last_squares()

        @block.scalar
        def _(act):
            def split_w(g):
                act.wait_ge(w_landed[g.slot], number((g.half + 1) * 16))
                if above_zero(g - 1):
                    act.wait_ge(tile_done, number(g - 1))
                act.activation(w_hi[:, g.slot, :], w_raw[:, g.slot, :], ACT.Copy).then_inc(w_hi_ready, 1)

            def norm(layer):
                for at, m in enumerate(M_ORDER):
                    if layer == 0:
                        act.wait_ge(x_landed[m], 16)
                    else:
                        act.wait_ge(residual_ready, number((layer - 1) * KT + at + 1))
                    if layer < 2:
                        act.activation(u_hi[:, m, :], h[:, m, :], ACT.Copy,
                                       scale=gain[:, layer * KT + m:layer * KT + m + 1]).then_inc(u_hi_ready, 1)
                    if at >= SQUARES and layer < 2:
                        act.wait_ge(squares_added, number(layer * (KT - 1) + max(at - SQUARES, 1)))
                    elif at >= SQUARES:
                        act.wait_ge(squares_used, number(at + 1 - SQUARES))
                    act.activation(square[:, at % SQUARES, :], h[:, m, :], ACT.Square).then_inc(squares_ready, 1)

            def root(out, sums, layer):
                act.wait_ge(sum_done, number(layer + 1))
                act.activation(out, sums, ACT.Sqrt, scale=1.0 / D_MODEL, bias=eps[:, 0:1]).then_inc(root_ready, 1)

            def rope_hi(r, out):
                act.wait_ge(rotated_ready, number(r + 1))
                act.activation(out, rotated[:, r.slot, :], ACT.Copy).then_inc(rope_hi_ready, 1)

            def relu(t):
                for s in range(2):
                    for kk, i in enumerate((3, 2, 1)):
                        act.wait_ge(idx_done, number(t * 6 + (3 * s + kk + 1)))
                        if above_zero(t * 6 + (3 * s + kk - 5)):
                            act.wait_ge(score_ready, number(t * 6 + (3 * s + kk - 5)))
                        at = OFF[i] - P
                        act.activation(rel[s][:, at:at + (i + 1) * P],
                                       ps[:, (S_BANK, T_BANK)[s] + i - 1, 0:(i + 1) * P],
                                       ACT.Relu).then_inc(rel_ready, 1)

            def v_part(vn):
                act.wait_ge(v_turned, number(vn + 1))
                act.activation(v_hi[:, :], ps[:, T_BANK + 1, :], ACT.Copy).then_inc(v_hi_ready, 1)

            def silu(z, row, n):
                act.wait_ge(bank_read[n.slot], number(n.half + 1))
                act.activation(gated[:, row.value, :], z_f[:, :], ACT.Silu).then_inc(silu_ready, 1)

            def exps(n):
                if above_zero(n * 3):
                    act.wait_ge(probs_turned, number(n * 3))
                for kk, i in enumerate((3, 2, 1, 0)):
                    act.wait_ge(scores_read, number(n * QB + (kk + 1)))
                    cols = slice(OFF[i], OFF[i] + (i + 1) * P)
                    act.activation(probs[:, cols], neg_s[:, cols], ACT.Exp, bias=neg_max[:, i:i + 1], scale=-1.0,
                                   accum_out=den[:, i:i + 1]).then_inc(exp_done, 1)

            def probs_hi(n):
                for b, (at, end) in enumerate(((0, T_OFF[1]), (T_OFF[1], T_OFF[2]), (T_OFF[2], COLS))):
                    act.wait_ge(probs_turned, number(n * 3 + (b + 1)))
                    act.activation(pT_hi[:, at:end], ps[:, T_BANK + b, 0:end - at],
                                   ACT.Copy).then_inc(pT_hi_ready, 1)

            def split_o(layer, t):
                act.wait_ge(gated_ready, number(t + (layer * HEADS + 1)))
                act.wait_ge(tile_done, number(t + (T_OUT[layer] - 1)))
                act.activation(o_hi[:, t.slot, :], gated[:, t.value, :], ACT.Copy).then_inc(o_hi_ready, 1)

            def head_a(h):
                attend, rope = (lo <= h.base < lo + HEADS or h.per for lo in (2, 1))
                if h.base < HEADS + LATE_GATES or h.per:
                    split_w(h + (T_Q + 1))
                if attend:
                    exps(h - 2)
                if rope:
                    rope_hi(h + (R_Q - 1), q_hi[:, (h.base - 1) % 2, :])
                if h.base > HEADS and not h.per:
                    silu(h - (LATE_GATES + 1), h - (LATE_GATES + 1), h + (T_Q - 1))
                if attend:
                    probs_hi(h - 2)

            def head_b(h):
                new, attend = h.base < HEADS or h.per, h.base > 0
                n, proj, tile, r = h + (HEADS - 1), h * 4 + PROJ_B, h * 4 + T_B, h * 2 + R_B
                if attend:
                    split_w(tile)
                    exps(n)
                if new and attend:
                    split_w(tile + 1)
                if attend:
                    silu(n, h - 1, proj - 1)
                    act.preload_act_table(ACT.Exp)
                if new and attend:
                    split_w(tile + 2)
                if attend:
                    probs_hi(n)
                if new:
                    rope_hi(r, q_hi[:, 0, :])
                    split_w(tile + 3)
                    rope_hi(r + 1, k_hi[:, :])
                    v_part(h + 1)

            def out_projections(layer):
                def step(t):
                    if t.base < HEADS - 1 or t.per:
                        split_w(t + (T_OUT[layer] + 1))
                        split_o(layer, t + 1)
                    elif layer == 0:
                        split_w(t + (T_OUT[layer] + 1))

                step(Count(0))
                with act.Fori(0, HEADS // 2 - 1) as i:
                    step(Count(1, 2, i))
                    step(Count(2, 2, i))
                step(Count(HEADS - 1))

            act.dma_start(gain[:, :], gains).then_inc(gain_landed, 16)
            act.preload_act_table(ACT.Sqrt)
            split_w(Count(0))
            act.wait_ge(gain_landed, 16)
            norm(0)
            split_w(Count(1))
            split_w(Count(2))
            act.wait_ge(eps_ready, 1)
            root(rstd[:, :], ps[:, S_BANK, :], 0)
            split_w(Count(3))
            act.wait_ge(ik_zeroed, 1)
            act.wait_ge(rotated_ready, 1)
            for s in range(2):
                for half in range(2):
                    to, of = slice(64 * half + 32 * s, 64 * half + 32 * s + 32), slice(64 * half, 64 * half + 32)
                    last = act.activation(ik[to, 2 * s, :], rotated[of, 0, :], ACT.Copy)
            last.then_inc(rope_hi_ready, 1)
            rope_hi(Count(R_IQ), q_hi[:, 0, :])
            act.preload_act_table(ACT.Silu)

            def idx_step(t):
                split_w(t + (T_IQ + 1))
                if t.base <= IDX_TILES or t.per:
                    rope_hi(t + (R_IQ - 1), q_hi[:, (t.base - 1) % 2, :])
                relu(t - 2)

            idx_step(Count(2))
            with act.Fori(0, IDX_TILES // 2 - 1) as i:
                idx_step(Count(3, 2, i))
                idx_step(Count(4, 2, i))
            idx_step(Count(IDX_TILES + 1))
            act.wait_ge(score_ready, 6 * IDX_TILES)
            act.activation(left, score[:, :], ACT.Copy).then_inc(left_ready, 1)
            split_w(Count(T_Z + 1))
            rope_hi(Count(R_K), k_hi[:, :])

            def gate_step(z):
                n = z + T_Z
                split_w(n + 1)
                silu(z, z, n)

            silu(Count(0), Count(0), Count(T_Z))
            v_part(Count(0))
            with act.Fori(0, EARLY_GATES // 2 - 1) as i:
                gate_step(Count(1, 2, i))
                gate_step(Count(2, 2, i))
            gate_step(Count(EARLY_GATES - 1))
            head_a(Count(0))
            act.preload_act_table(ACT.Exp)
            for h0 in range(1, 3):
                head_a(Count(h0))
            with act.Fori(0, HEADS // 2 - 2) as i:
                head_a(Count(3, 2, i))
                head_a(Count(4, 2, i))
            for h0 in range(HEADS - 1, HEADS + 2):
                head_a(Count(h0))
            split_o(0, Count(0))
            head_a(Count(HEADS + 2))
            out_projections(0)
            act.preload_act_table(ACT.Sqrt)
            norm(1)
            split_w(Count(T_B + 1))
            split_w(Count(T_B + 2))
            root(rstd[:, :], ps[:, S_BANK, :], 1)
            act.preload_act_table(ACT.Exp)
            head_b(Count(0))
            with act.Fori(0, HEADS - 1) as i:
                head_b(Count(1, 1, i))
            head_b(Count(HEADS))
            split_o(1, Count(0))
            out_projections(1)
            act.preload_act_table(ACT.Sqrt)
            norm(2)
            root(root_turned[:, :], ps[:, 0, 0:QB], 2)

        @block.vector
        def _(dve):
            def norm(layer):
                for at, m in enumerate(M_ORDER):
                    if layer:
                        if at < KT - 1:
                            dve.wait_ge(y_done, number((layer - 1) * (KT - 1) + at + 1))
                        else:
                            dve.wait_ge(tile_done, number(T_OUT[layer - 1] + HEADS))
                        dve.tensor_tensor(h[:, m, :], ps[:, m, :], h[:, m, :], ALU.add).then_inc(residual_ready, 1)
                    if layer < 2 and at:
                        u_part(layer, at - 1)
                if layer < 2:
                    u_part(layer, KT - 1)

            def u_part(layer, at):
                m = M_ORDER[at]
                dve.wait_ge(u_hi_ready, number(layer * KT + at + 1))
                dve.scalar_tensor_tensor(out=u_lo[:, m, :], in0=h[:, m, :],
                                         scalar=gain[:, layer * KT + m:layer * KT + m + 1],
                                         in1=u_hi[:, m, :].bitcast(F32), op0=ALU.mult,
                                         op1=ALU.subtract).then_inc(u_lo_ready, 1)

            def split_w(g):
                dve.wait_ge(w_hi_ready, number(g + 1))
                dve.tensor_tensor(w_lo[:, g.slot, :], w_raw[:, g.slot, :], w_hi[:, g.slot, :].bitcast(F32),
                                  ALU.subtract).then_inc(w_lo_ready, 1)

            def invert_root(layer):
                dve.wait_ge(root_ready, number(layer + 1))
                dve.reciprocal(rstd[:, :], rstd[:, :]).then_inc(rstd_ready, 1)
                dve.wait_ge(rstd_ready, number(layer + 1))

            def scale_tables(layer):
                for s in range(2):
                    dve.tensor_tensor(scaled[:, s, :], table[:, s, :], rstd[:, :], ALU.mult).then_inc(tables_scaled, 1)
                dve.wait_ge(tables_scaled, number(2 * layer + 2))

            def scale_values(n, g):
                dve.wait_ge(tile_done, number(g + 1))
                dve.tensor_tensor(v_f[:, :], ps[:, n.slot, :], rstd[:, :], ALU.mult).then_inc(bank_read[n.slot], 1)

            def scale_gate(z, n, g):
                dve.wait_ge(tile_done, number(g + 1))
                if above_zero(z):
                    dve.wait_ge(silu_ready, number(z))
                dve.tensor_tensor(z_f[:, :], ps[:, n.slot, :], rstd[:, :], ALU.mult).then_inc(bank_read[n.slot], 1)

            def first_rope(n, g, cos):
                dve.wait_ge(tile_done, number(g + 1))
                half = P // 2
                dve.tensor_tensor(by_sin[0:half, :], ps[half:P, n.slot, :], table[half:P, cos + 1, :], ALU.mult)
                dve.tensor_tensor(by_sin[half:P, :], ps[0:half, n.slot, :], table[0:half, cos + 1, :], ALU.mult)
                dve.tensor_tensor(by_cos[:, :], ps[:, n.slot, :], table[:, cos, :], ALU.mult).then_inc(
                    bank_read[n.slot], 1)
                dve.wait_ge(bank_read[n.slot], number(n.half + 1))
                dve.tensor_tensor(rotated[:, 0, :], by_cos[:, :], by_sin[:, :], ALU.add).then_inc(first_ready, 1)

            def scale_first(layer):
                dve.wait_ge(first_ready, layer + 1)
                dve.tensor_tensor(rotated[:, 0, :], rotated[:, 0, :], rstd[:, :], ALU.mult).then_inc(rotated_ready, 1)

            def rope(r, n, g, of=scaled, cos=0):
                dve.wait_ge(tile_done, number(g + 1))
                if above_zero(r):
                    dve.wait_ge(rotated_ready, number(r))
                raw, half = ps[:, n.slot, :], P // 2
                dve.tensor_tensor(by_sin[0:half, :], ps[half:P, n.slot, :], of[half:P, cos + 1, :], ALU.mult)
                dve.tensor_tensor(by_sin[half:P, :], ps[0:half, n.slot, :], of[0:half, cos + 1, :], ALU.mult)
                dve.tensor_tensor(by_cos[:, :], raw, of[:, cos, :], ALU.mult).then_inc(bank_read[n.slot], 1)
                dve.wait_ge(bank_read[n.slot], number(n.half + 1))
                if above_zero(r - 1):
                    dve.wait_ge(rope_lo_ready, number(r - 1))
                dve.tensor_tensor(rotated[:, r.slot, :], by_cos[:, :], by_sin[:, :],
                                  ALU.add).then_inc(rotated_ready, 1)

            def add_scores(t):
                for s in range(2):
                    for kk, i in enumerate((3, 2, 1)):
                        dve.wait_ge(rel_ready, number(t * 6 + (3 * s + kk + 1)))
                        if above_zero(t * 6 + (3 * s + kk - 2)):
                            dve.wait_ge(score_ready, number(t * 6 + (3 * s + kk - 2)))
                        cols = slice(OFF[i] - P, OFF[i] + i * P)
                        head = (t * 2 + s).value
                        dve.scalar_tensor_tensor(out=score[:, cols], in0=rel[s][:, cols],
                                                 scalar=iw[:, i - 1, bass.ds(head, 1)], in1=score[:, cols],
                                                 op0=ALU.mult, op1=ALU.add).then_inc(score_ready, 1)

            def take_eight(r):
                for i in range(1, QB):
                    if above_zero(r * 3 + (i - 3)):
                        least = in_register(dve, r * 3 + (i - 3))
                        dve.wait_ge(top8_taken, 1)
                        dve.wait_ge(top8_taken, least)
                    dve.max(top8[:, i - 1, :], left[:, OFF[i] - P:OFF[i] + i * P]).then_inc(top8_ready, 1)
                for i in range(1, QB):
                    least = in_register(dve, r * 3 + i)
                    dve.wait_ge(top8_ready, 1)
                    dve.wait_ge(top8_ready, least)
                    part = left[:, OFF[i] - P:OFF[i] + i * P]
                    dve.match_replace(part, top8[:, i - 1, :], part, NEG).then_inc(top8_taken, 1)

            def mask_scores(n, bias, offset):
                for kk, i in enumerate((3, 2, 1, 0)):
                    if i:
                        if above_zero(n * QB + (kk + 1 - QB)):
                            dve.wait_ge(exp_done, number(n * QB + (kk + 1 - QB)))
                        least = in_register(dve, n * 3 + (kk + 1))
                        dve.wait_ge(scores_done, 1)
                        dve.wait_ge(scores_done, least)
                    else:
                        if above_zero(n * QB):
                            least = in_register(dve, n * QB)
                            dve.wait_ge(exp_done, 1)
                            dve.wait_ge(exp_done, least)
                    at = 2 * P if i == 0 else 0
                    width = (i + 1) * P
                    dve.tensor_tensor_reduce(neg_s[:, OFF[i]:OFF[i] + width],
                                             ps[:, S_BANK + max(i, 1) - 1, at:at + width],
                                             bias[:, offset(i):offset(i) + width], -SCALE, -NEG, ALU.add, ALU.min,
                                             neg_max[:, i:i + 1]).then_inc(scores_read, 1)

            def invert(n):
                dve.wait_ge(exp_done, number(n * QB + QB))
                dve.reciprocal(inv_den[:, :], den[:, :]).then_inc(inv_ready, 1)

            def probs_lo(n):
                for b, (at, end) in enumerate(((0, T_OFF[1]), (T_OFF[1], T_OFF[2]), (T_OFF[2], COLS))):
                    dve.wait_ge(pT_hi_ready, number(n * 3 + (b + 1)))
                    dve.tensor_tensor(pT_lo[:, at:end], ps[:, T_BANK + b, 0:end - at],
                                      pT_hi[:, at:end].bitcast(F32), ALU.subtract).then_inc(pT_lo_ready, 1)

            def v_part(vn):
                dve.wait_ge(v_hi_ready, number(vn + 1))
                dve.tensor_tensor(v_lo[:, :], ps[:, T_BANK + 1, :], v_hi[:, :].bitcast(F32),
                                  ALU.subtract).then_inc(v_lo_ready, 1)

            def gate(n, row):
                dve.wait_ge(o_done, number(n + 1))
                dve.wait_ge(silu_ready, number(n + 1))
                dve.tensor_tensor(gated[:, row.value, :], ps[:, T_BANK, :], gated[:, row.value, :],
                                  ALU.mult).then_inc(gated_ready, 1)

            def head_a(h):
                attend, roped, finish = (lo <= h.base < lo + HEADS or h.per for lo in (2, 1, 3))
                if attend:
                    mask_scores(h - 2, bias_a, lambda i: OFF[i])
                if roped:
                    rope(h + (R_Q - 1), h + (T_Q - 1), h + (T_Q - 1))
                if attend:
                    invert(h - 2)
                if h.base > HEADS and not h.per:
                    scale_gate(h - (LATE_GATES + 1), h + (T_Q - 1), h + (T_Q - 1))
                if finish:
                    gate(h - 3, h - 3)
                if attend:
                    probs_lo(h - 2)

            def head_b(h):
                new, attend = h.base < HEADS or h.per, h.base > 0
                n, proj, tile, r = h + (HEADS - 1), h * 4 + PROJ_B, h * 4 + T_B, h * 2 + R_B
                if attend:
                    mask_scores(n, bias_b, lambda i: SEQ - (i + 1) * P)
                    invert(n)
                    scale_gate(n, proj - 1, tile - 1)
                if new and attend:
                    rope(r, proj, tile)
                if attend:
                    probs_lo(n)
                if new:
                    rope(r + 1, proj + 1, tile + 1)
                if new:
                    scale_values(proj + 2, tile + 2)
                if attend:
                    gate(n, h - 1)
                if new:
                    v_part(h + 1)

            dve.memset(ones[:, :], 1.0).then_inc(ones_ready, 1)
            dve.memset(eps[:, :], NORM_EPS).then_inc(eps_ready, 1)
            split_w(Count(0))
            dve.wait_ge(gain_landed, 16)
            norm(0)
            split_w(Count(1))
            dve.wait_ge(tile_done, 1)
            dve.tensor_scalar(iwT[:, :], ps[32:32 + IDX_HEADS, 0, :], IDX_SCALE, None, ALU.mult).then_inc(iwT_raw, 1)
            dve.wait_ge(table_landed, 16 * 3)
            first_rope(Count(0), Count(0), cos=2)
            invert_root(0)
            dve.wait_ge(iwT_raw, 1)
            dve.tensor_tensor(iwT[:, :], iwT[:, :], rstd[0:IDX_HEADS, :], ALU.mult).then_inc(iwT_ready, 1)
            scale_first(0)
            for s in range(2):
                dve.tensor_tensor(table[:, 2 + s, :], table[:, 2 + s, :], rstd[:, :], ALU.mult).then_inc(idx_scaled, 1)
            dve.wait_ge(idx_scaled, 2)
            rope(Count(R_IQ), Count(T_IQ), Count(T_IQ), of=table, cos=2)
            dve.wait_ge(iw_turned, 1)
            dve.tensor_copy(iw[:, :, :], ps[:, T_BANK, 0:(QB - 1) * IDX_HEADS].rearrange(
                "p (i n) -> p i n", n=IDX_HEADS)).then_inc(iw_ready, 1)
            dve.wait_ge(rope_hi_ready, 1)
            for s in range(2):
                for half in range(2):
                    to, of = slice(64 * half + 32 * s, 64 * half + 32 * s + 32), slice(64 * half, 64 * half + 32)
                    last = dve.tensor_tensor(ik[to, 2 * s + 1, :], rotated[of, 0, :], ik[of, 0, :].bitcast(F32),
                                             ALU.subtract)
            last.then_inc(rope_lo_ready, 1)
            dve.wait_ge(iw_ready, 1)
            dve.wait_ge(score_zeroed, 2)

            def idx_step(t):
                rope(t + (R_IQ - 1), t + (T_IQ - 1), t + (T_IQ - 1), of=table, cos=2)
                add_scores(t - 2)

            idx_step(Count(2))
            with dve.Fori(0, IDX_TILES // 2 - 1) as i:
                idx_step(Count(3, 2, i))
                idx_step(Count(4, 2, i))
            scale_values(Count(T_V), Count(T_V))
            add_scores(Count(IDX_TILES - 1))
            scale_tables(0)
            rope(Count(R_K), Count(T_K), Count(T_K))
            dve.wait_ge(left_ready, 1)
            take_eight(Count(0))

            def gate_step(z):
                scale_gate(z, z + T_Z, z + T_Z)
                take_eight(z + 1)

            gate_step(Count(0))
            v_part(Count(0))
            with dve.Fori(0, EARLY_GATES // 2 - 1) as i:
                gate_step(Count(1, 2, i))
                gate_step(Count(2, 2, i))
            gate_step(Count(EARLY_GATES - 1))
            for r in range(EARLY_GATES + 1, TOP_K // 8):
                take_eight(Count(r))
            dve.wait_ge(top8_taken, 3 * TOP_K // 8)
            dve.tensor_tensor(bias_a[:, P:COLS], score[:, :], left, ALU.is_gt).then_inc(chosen_ready, 1)
            dve.wait_ge(chosen_ready, 1)
            dve.tensor_scalar(bias_a[:, P:COLS], bias_a[:, P:COLS], -1.0, -NEG, ALU.add,
                              ALU.mult).then_inc(bias_ready, 1)
            dve.wait_ge(bias_ready, 1)
            dve.wait_ge(bias_landed, 32)
            for h0 in range(3):
                head_a(Count(h0))
            with dve.Fori(0, HEADS // 2 - 2) as i:
                head_a(Count(3, 2, i))
                head_a(Count(4, 2, i))
            for h0 in range(HEADS - 1, HEADS + 3):
                head_a(Count(h0))
            norm(1)
            split_w(Count(T_B + 1))
            first_rope(Count(PROJ_B), Count(T_B), cos=0)
            invert_root(1)
            scale_first(1)
            scale_tables(1)
            head_b(Count(0))
            with dve.Fori(0, HEADS - 1) as i:
                head_b(Count(1, 1, i))
            head_b(Count(HEADS))
            norm(2)
            dve.wait_ge(root_ready, 3)
            dve.reciprocal(inv_turned[:, :], root_turned[:, :]).then_inc(inv_turned_ready, 1)
            dve.wait_ge(inv_turned_ready, 1)
            for i in range(QB):
                dve.tensor_scalar(square_sum[:, i * P:(i + 1) * P], ident[:, :], inv_turned[:, i:i + 1], None,
                                  ALU.mult).then_inc(diagonal_ready, 1)
            dve.wait_ge(spread_done, 1)
            dve.tensor_copy(rstd[:, :], ps[:, 1, :]).then_inc(rstd_ready, 1)
            dve.wait_ge(rstd_ready, 3)
            for at, m in enumerate(M_ORDER):
                if at not in POOL_OUT:
                    dve.scalar_tensor_tensor(out=h[:, m, :], in0=h[:, m, :], scalar=gain[:, 2 * KT + m:2 * KT + m + 1],
                                             in1=rstd[:, :], op0=ALU.mult, op1=ALU.mult).then_inc(out_dve, 1)

        @block.gpsimd
        def _(pool):
            def split_w(g):
                pool.wait_ge(w_hi_ready, number(g + 1))
                pool.tensor_tensor(w_lo[:, g.slot, :], w_raw[:, g.slot, :], w_hi[:, g.slot, :].bitcast(F32),
                                   ALU.subtract).then_inc(w_lo_ready, 1)

            def add_squares(layer):
                for at in range(1, KT):
                    pool.wait_ge(squares_ready, number(layer * KT + at + 1))
                    if at > 1:
                        pool.wait_ge(squares_added, number(layer * (KT - 1) + at - 1))
                    so_far = square[:, 0, :] if at == 1 else square_sum[:, :]
                    pool.tensor_tensor(square_sum[:, :], so_far, square[:, at % SQUARES, :],
                                       ALU.add).then_inc(squares_added, 1)

            def rope_lo(r, hi, lo):
                pool.wait_ge(rope_hi_ready, number(r + 1))
                pool.tensor_tensor(lo, rotated[:, r.slot, :], hi.bitcast(F32), ALU.subtract).then_inc(rope_lo_ready, 1)

            def normalise(n):
                least = in_register(pool, n + 1)
                pool.wait_ge(inv_ready, 1)
                pool.wait_ge(inv_ready, least)
                for i in (3, 2, 1, 0):
                    cols = slice(OFF[i], OFF[i] + (i + 1) * P)
                    pool.tensor_scalar(probs[:, cols], probs[:, cols], inv_den[:, i:i + 1], 1.0, ALU.mult,
                                       ALU.mult).then_inc(probs_ready, 1)

            def split_o(layer, t):
                pool.wait_ge(o_hi_ready, number(t + (layer * HEADS + 1)))
                pool.tensor_tensor(o_lo[:, t.slot, :], gated[:, t.value, :], o_hi[:, t.slot, :].bitcast(F32),
                                   ALU.subtract).then_inc(o_lo_ready, 1)

            def head_a(h):
                attend, rope = (lo <= h.base < lo + HEADS or h.per for lo in (2, 1))
                if h.base < HEADS + LATE_GATES or h.per:
                    split_w(h + (T_Q + 1))
                if attend:
                    normalise(h - 2)
                if rope:
                    slot = (h.base - 1) % 2
                    rope_lo(h + (R_Q - 1), q_hi[:, slot, :], q_lo[:, slot, :])

            def head_b(h):
                new, attend = h.base < HEADS or h.per, h.base > 0
                tile, r = h * 4 + T_B, h * 2 + R_B
                if attend:
                    split_w(tile)
                    normalise(h + (HEADS - 1))
                if attend and new:
                    split_w(tile + 1)
                if new:
                    split_w(tile + 2)
                    rope_lo(r, q_hi[:, 0, :], q_lo[:, 0, :])
                    split_w(tile + 3)
                    rope_lo(r + 1, k_hi[:, :], k_lo[:, :])

            def out_projections(layer):
                def step(t):
                    if t.base < HEADS - 1 or t.per:
                        split_w(t + (T_OUT[layer] + 1))
                        split_o(layer, t + 1)
                    elif layer == 0:
                        split_w(t + (T_OUT[layer] + 1))

                step(Count(0))
                with pool.Fori(0, HEADS // 2 - 1) as i:
                    step(Count(1, 2, i))
                    step(Count(2, 2, i))
                step(Count(HEADS - 1))

            pool.memset(ik[:, :, :].bitcast(F32), 0.0).then_inc(ik_zeroed, 1)
            pool.memset(score[:, :], 0.0).then_inc(score_zeroed, 1)
            add_squares(0)
            pool.wait_ge(score_zeroed, 1)
            pool.wait_ge(bias_landed, 32)
            for i in range(1, QB):
                last = pool.tensor_copy(score[:, OFF[i] - P + i * P:OFF[i] + i * P], bias_a[:, 0:P])
            last.then_inc(score_zeroed, 1)

            def idx_step(t):
                split_w(t + (T_IQ + 1))
                rope_lo(t + (R_IQ - 1), q_hi[:, (t.base - 1) % 2, :], q_lo[:, (t.base - 1) % 2, :])

            pool.wait_ge(w_lo_ready, 2)
            split_w(Count(T_IQ + 1))
            split_w(Count(T_IQ + 2))
            pool.wait_ge(rope_lo_ready, 1)
            rope_lo(Count(R_IQ), q_hi[:, 0, :], q_lo[:, 0, :])
            with pool.Fori(0, IDX_TILES // 2 - 1) as i:
                idx_step(Count(2, 2, i))
                idx_step(Count(3, 2, i))
            idx_step(Count(IDX_TILES))
            split_w(Count(T_Z))
            split_w(Count(T_Z + 1))
            rope_lo(Count(R_K), k_hi[:, :], k_lo[:, :])
            with pool.Fori(0, EARLY_GATES // 2 - 1) as i:
                split_w(Count(T_Z + 2, 2, i))
                split_w(Count(T_Z + 3, 2, i))
            split_w(Count(T_Q))
            for h0 in range(3):
                head_a(Count(h0))
            with pool.Fori(0, HEADS // 2 - 2) as i:
                head_a(Count(3, 2, i))
                head_a(Count(4, 2, i))
            for h0 in range(HEADS - 1, HEADS + 3):
                head_a(Count(h0))
            split_o(0, Count(0))
            out_projections(0)
            add_squares(1)
            pool.wait_ge(w_lo_ready, T_B + 2)
            head_b(Count(0))
            with pool.Fori(0, HEADS - 1) as i:
                head_b(Count(1, 1, i))
            head_b(Count(HEADS))
            split_o(1, Count(0))
            out_projections(1)
            pool.wait_ge(rstd_ready, 3)
            for m in (M_ORDER[at] for at in POOL_OUT):
                pool.tensor_tensor(h[:, m, :], h[:, m, :], rstd[:, :], ALU.mult).then_inc(out_half, 1)
                pool.wait_ge(out_half, POOL_OUT.index(M_ORDER.index(m)) + 1)
                pool.tensor_scalar(h[:, m, :], h[:, m, :], gain[:, 2 * KT + m:2 * KT + m + 1], 1.0, ALU.mult,
                                   ALU.mult).then_inc(out_pool, 1)


def rotary_table(rows_per_head, sin):
    dim = 2 * rows_per_head
    freqs = np.float32(10000.0) ** (-np.arange(0, dim, 2, dtype=np.float32) / np.float32(dim))
    angle = np.arange(SEQ, dtype=np.float32)[None, :] * freqs[np.arange(P) % rows_per_head][:, None]
    if not sin:
        return np.cos(angle)
    return np.sin(angle) * np.where(np.arange(P) < P // 2, 1, -1).astype(np.float32)[:, None]


def constants():
    dist = np.arange(P)[:, None] - (np.arange(SEQ)[None, :] - (SEQ - P))
    times = sum(((dist >= 0) & (dist <= window) & (dist % dilation == 0)).astype(np.float64)
                for window, dilation in CONFIGS)
    dilated = np.where(times > 0, np.log(np.maximum(times, 1)) / SCALE, NEG).astype(np.float32)
    causal = np.where(np.arange(P)[:, None] >= np.arange(P)[None, :], 0, NEG).astype(np.float32)
    tables = np.stack([rotary_table(64, False), rotary_table(64, True), rotary_table(32, False),
                       rotary_table(32, True)], 1)
    return tables.astype(np.float32), dilated, causal, np.eye(P, dtype=np.float32)


def tiles_of(w):
    n = w.shape[1] // P
    return w.reshape(KT, P, n, P).transpose(2, 1, 0, 3).reshape(n, P, D_MODEL)


def kernel(**inputs):
    from concourse import bacc
    from concourse.bass_utils import run_bass_kernel_spmd

    a_in, b_in = np.asarray(inputs["a_w_in"])[0], np.asarray(inputs["b_w_in"])[0]
    ends = np.cumsum([D_INNER, HEAD_DIM, HEAD_DIM, IDX_HEADS * IDX_DIM, IDX_DIM, IDX_HEADS])
    aq, ak, av, aiq, aik, aiw, az = np.split(a_in, ends, axis=1)
    half = IDX_DIM // 2
    first = np.zeros((D_MODEL, P), a_in.dtype)
    first[:, 0:half], first[:, 64:64 + half] = aik[:, :half], aik[:, half:]
    first[:, half:half + IDX_HEADS] = aiw
    aiq = aiq.reshape(D_MODEL, IDX_TILES, 2, 2, half).transpose(0, 1, 3, 2, 4).reshape(D_MODEL, IDX_HEADS * IDX_DIM)
    b_in = b_in.reshape(D_MODEL, 4, HEADS, HEAD_DIM).transpose(0, 2, 1, 3).reshape(D_MODEL, 4 * D_INNER)
    weights = np.concatenate(
        [tiles_of(first), tiles_of(aiq), tiles_of(av), tiles_of(ak), tiles_of(az)[:EARLY_GATES], tiles_of(aq),
         tiles_of(az)[EARLY_GATES:], np.asarray(inputs["a_w_out"])[0].reshape(HEADS, P, D_MODEL), tiles_of(b_in),
         np.asarray(inputs["b_w_out"])[0].reshape(HEADS, P, D_MODEL)])
    gains = np.concatenate([np.asarray(inputs["norm_g"]), np.asarray(inputs["final_g"])[None]])
    gains = gains.reshape(3, KT, P).transpose(2, 0, 1).reshape(P, 3 * KT)
    tables, dilated, causal, ident = constants()
    arrays = {
        "x_turned": np.asarray(inputs["x"])[0].T, "gains": gains, "weights": weights, "rope_tables": tables,
        "dilated_bias": dilated, "causal_bias": causal, "identity": ident,
    }
    arrays = {name: np.ascontiguousarray(a) for name, a in arrays.items()}
    nc = bacc.Bacc("TRN2", target_bir_lowering=False, num_devices=1)
    args = [nc.dram_tensor(name, a.shape, mybir.dt.from_np(a.dtype), kind="ExternalInput").ap()
            for name, a in arrays.items()]
    args.append(nc.dram_tensor("outT", (D_MODEL, SEQ), F32, kind="ExternalOutput").ap())
    build(nc, *args)
    r = run_bass_kernel_spmd(nc, [arrays], core_ids=[0])
    return np.asarray(r.results[0]["outT"]).T.reshape(1, SEQ, D_MODEL)
```

```python
from contextlib import ExitStack

import numpy as np

import concourse.bass as bass
from concourse import mybir

F32 = mybir.dt.float32
F32R = mybir.dt.float32r
ALU = mybir.AluOpType
ACT = mybir.ActivationFunctionType

P = 128
D_MODEL, SEQ, D_INNER = 1024, 512, 2048
KT = D_MODEL // P
QB = SEQ // P
HEADS, HEAD_DIM = 16, 128
IDX_HEADS, IDX_DIM = 16, 64
IDX_TILES = IDX_HEADS * IDX_DIM // P
TOP_K = min(256, SEQ // 4)
NORM_EPS = 1e-6
SCALE = HEAD_DIM ** -0.5
IDX_SCALE = IDX_HEADS ** -0.5 * IDX_DIM ** -0.5
NEG = -3e38
CONFIGS = ((128, 1), (512, 4), (2048, 16))

OFF = [P * i * (i + 1) // 2 for i in range(QB)]
COLS = P * QB * (QB + 1) // 2
T_OFF = [0, SEQ, SEQ + 3 * P, SEQ + 5 * P]

T_IK, T_IQ, T_V, T_K, T_Z = 0, 1, 1 + IDX_TILES, 2 + IDX_TILES, 3 + IDX_TILES
LATE_GATES = 2
EARLY_GATES = HEADS - LATE_GATES
assert (EARLY_GATES - 2) % 4 == 0
T_Q = T_Z + EARLY_GATES
T_LATE = T_Q + HEADS
T_OUT = [T_LATE + LATE_GATES, T_LATE + LATE_GATES + HEADS + 4 * HEADS]
T_B = T_OUT[0] + HEADS
TILES = T_OUT[1] + HEADS
PROJ_B = T_OUT[0]
R_IQ, R_K = 1, 1 + IDX_TILES
R_Q = R_K + 1
R_B = R_Q + HEADS
assert TOP_K == P == 8 * HEADS and T_OFF[-1] + P == COLS

ALL = slice(0, SEQ)
CHOOSING = slice(TOP_K, SEQ)

M_ORDER = (0, 1, 2, 3, 4, 6, 7, 5)
POOL_OUT = (2, 5)
SQUARES = 3
POOL_SQUARES = 5
S_BANK, T_BANK = 2, 5


class Count:

    def __init__(self, base, per=0, turn=None):
        self.base, self.per, self.turn = base, per, turn

    def __add__(self, k):
        return Count(self.base + k, self.per, self.turn)

    def __sub__(self, k):
        return self + (-k)

    def __mul__(self, k):
        return Count(self.base * k, self.per * k, self.turn)

    @property
    def value(self):
        return self.turn * self.per + self.base if self.per else self.base

    @property
    def slot(self):
        assert self.per % 2 == 0
        return self.base % 2

    @property
    def half(self):
        assert self.per % 2 == 0
        return Count(self.base // 2, self.per // 2, self.turn)


def number(count):
    return count.value if isinstance(count, Count) else count


def above_zero(count):
    return (count.base if isinstance(count, Count) else count) > 0


def in_register(eng, count):
    return eng.to_reg(count.value) if count.per else count.base


def build(nc, xT, gains, weights, rope_tables, dilated_bias, causal_bias, ident_in, outT):
    with ExitStack() as ctx:
        def sb(name, shape, dt=F32):
            return ctx.enter_context(nc.sbuf_tensor(name, shape, dt))

        def sem(name):
            return ctx.enter_context(nc.semaphore(name))

        ps = ctx.enter_context(nc.psum_tensor("ps", [P, 8, SEQ], F32))

        w_raw = sb("w_raw", [P, 2, D_MODEL])
        w_hi = sb("w_hi", [P, 2, D_MODEL], F32R)
        w_lo = sb("w_lo", [P, 2, D_MODEL], F32R)
        h = sb("h", [P, KT, SEQ])
        u_hi = sb("u_hi", [P, KT, SEQ], F32R)
        u_lo = sb("u_lo", [P, KT, SEQ], F32R)
        gain = sb("gain", [P, 3 * KT])
        square = sb("square", [P, SQUARES, SEQ])
        square_sum = sb("square_sum", [P, SEQ])
        rstd = sb("rstd", [P, SEQ])
        root_turned = sb("root_turned", [P, QB])
        inv_turned = sb("inv_turned", [P, QB])
        eps = sb("eps", [P, 1])
        ones = sb("ones", [P, P])
        ident = sb("ident", [P, P])
        table = sb("table", [P, 4, SEQ])
        scaled = sb("scaled", [P, 2, SEQ])
        by_cos = sb("by_cos", [P, SEQ])
        by_sin = sb("by_sin", [P, SEQ])
        rotated = sb("rotated", [P, 2, SEQ])
        q_hi = sb("q_hi", [P, 2, SEQ], F32R)
        q_lo = sb("q_lo", [P, 2, SEQ], F32R)
        k_hi = sb("k_hi", [P, SEQ], F32R)
        k_lo = sb("k_lo", [P, SEQ], F32R)
        v_f = sb("v_f", [P, SEQ])
        v_hi = sb("v_hi", [P, SEQ], F32R)
        v_lo = sb("v_lo", [P, SEQ], F32R)
        bias_a = sb("bias_a", [P, COLS])
        bias_b = sb("bias_b", [P, SEQ])
        neg_s = sb("neg_s", [P, COLS])
        neg_max = sb("neg_max", [P, QB])
        probs = sb("probs", [P, COLS])
        den = sb("den", [P, QB])
        inv_den = sb("inv_den", [P, QB])
        pT_hi = sb("pT_hi", [P, COLS], F32R)
        pT_lo = sb("pT_lo", [P, COLS], F32R)
        z_f = sb("z_f", [P, SEQ])
        gated = sb("gated", [P, HEADS, SEQ])
        last_square = gated[:, 0:KT, :]
        o_hi = sb("o_hi", [P, 2, SEQ], F32R)
        o_lo = sb("o_lo", [P, 2, SEQ], F32R)
        ik = sb("ik", [P, 4, SEQ], F32R)
        iwT = sb("iwT", [IDX_HEADS, SEQ])
        iw = sb("iw", [P, QB - 1, IDX_HEADS])
        rel = [neg_s[:, 0:COLS - P], probs[:, 0:COLS - P]]
        score = sb("score", [P, COLS - P])
        left = rel[0]
        top8 = sb("top8", [P, QB - 1, 8])

        x_landed = [sem(f"x_landed{m}") for m in range(KT)]
        gain_landed, table_landed, bias_landed = sem("gain_landed"), sem("table_landed"), sem("bias_landed")
        w_landed = [sem("w_landed0"), sem("w_landed1")]
        w_hi_ready, w_lo_ready, tile_done = sem("w_hi_ready"), sem("w_lo_ready"), sem("tile_done")
        ones_ready, squares_ready, squares_added = sem("ones_ready"), sem("squares_ready"), sem("squares_added")
        sum_done, root_ready, rstd_ready = sem("sum_done"), sem("root_ready"), sem("rstd_ready")
        idx_scaled, tables_scaled = sem("idx_scaled"), sem("tables_scaled")
        u_hi_ready, u_lo_ready = sem("u_hi_ready"), sem("u_lo_ready")
        ik_hi_ready, ik_lo_ready = sem("ik_hi_ready"), sem("ik_lo_ready")
        iwT_raw, first_ready = sem("iwT_raw"), sem("first_ready")
        inv_turned_ready, diagonal_ready, spread_done = (
            sem("inv_turned_ready"), sem("diagonal_ready"), sem("spread_done"))
        silu_ready, eps_ready = sem("silu_ready"), sem("eps_ready")
        out_dve, out_half, out_pool = sem("out_dve"), sem("out_half"), sem("out_pool")
        bank_read = [sem("bank_read0"), sem("bank_read1")]
        rotated_ready = sem("rotated_ready")
        rope_hi_ready, rope_lo_ready = sem("rope_hi_ready"), sem("rope_lo_ready")
        ik_zeroed, iwT_ready, iw_turned, iw_ready = (
            sem("ik_zeroed"), sem("iwT_ready"), sem("iw_turned"), sem("iw_ready"))
        idx_done, rel_ready, score_ready = sem("idx_done"), sem("rel_ready"), sem("score_ready")
        score_zeroed, left_ready, top8_ready, top8_taken = (
            sem("score_zeroed"), sem("left_ready"), sem("top8_ready"), sem("top8_taken"))
        chosen_ready, bias_ready = sem("chosen_ready"), sem("bias_ready")
        v_turned, v_hi_ready, v_lo_ready = sem("v_turned"), sem("v_hi_ready"), sem("v_lo_ready")
        scores_done, scores_read, exp_done, inv_ready, probs_ready = (
            sem("scores_done"), sem("scores_read"), sem("exp_done"), sem("inv_ready"), sem("probs_ready"))
        probs_turned, pT_hi_ready, pT_lo_ready, o_done, gated_ready = (
            sem("probs_turned"), sem("pT_hi_ready"), sem("pT_lo_ready"), sem("o_done"), sem("gated_ready"))
        o_lo_ready, o_hi_ready, y_done, residual_ready = (
            sem("o_lo_ready"), sem("o_hi_ready"), sem("y_done"), sem("residual_ready"))
        out_stored = sem("out_stored")

        block = ctx.enter_context(nc.Block())

        @block.sync
        def _(sp):
            def load_tile(g):
                if above_zero(g - 1):
                    sp.wait_ge(w_lo_ready, number(g - 1))
                sp.dma_start(w_raw[:, g.slot, :], weights[g.value]).then_inc(w_landed[g.slot], 16)

            load_tile(Count(0))
            for m in M_ORDER:
                sp.dma_start(h[:, m, :], xT[m * P:(m + 1) * P, :]).then_inc(x_landed[m], 16)
            load_tile(Count(1))
            sp.dma_start(ident[:, :], ident_in).then_inc(table_landed, 16)
            sp.dma_start(table[:, 2:4, :], rope_tables[:, 2:4, :]).then_inc(table_landed, 16)
            sp.dma_start(table[:, 0:2, :], rope_tables[:, 0:2, :]).then_inc(table_landed, 16)
            sp.dma_start(bias_a[:, 0:P], causal_bias).then_inc(bias_landed, 16)
            sp.dma_start(bias_b[:, :], dilated_bias).then_inc(bias_landed, 16)
            with sp.Fori(0, TILES // 2 - 1) as i:
                load_tile(Count(2, 2, i))
                load_tile(Count(3, 2, i))
            for g in range(TILES // 2 * 2, TILES):
                load_tile(Count(g))
            for at, m in enumerate(M_ORDER):
                if at in POOL_OUT:
                    sp.wait_ge(out_pool, POOL_OUT.index(at) + 1)
                else:
                    sp.wait_ge(out_dve, at + 1 - sum(p < at for p in POOL_OUT))
                sp.dma_start(outT[m * P:(m + 1) * P, :], h[:, m, :]).then_inc(out_stored, 16)
            sp.wait_ge(out_stored, 16 * KT)

        @block.tensor
        def _(pe):
            def sum_squares(layer):
                pe.wait_ge(squares_added, number((layer + 1) * (KT - 1)))
                pe.matmul(ps[:, S_BANK, :], ones[:, :], square_sum[:, :], start=True, stop=True).then_inc(sum_done, 1)

            def sum_last_squares():
                for at in range(POOL_SQUARES, KT + 1):
                    if at < KT:
                        pe.wait_ge(squares_ready, 2 * KT + at + 1)
                        of = last_square[:, at, :]
                    else:
                        pe.wait_ge(squares_added, 2 * (KT - 1) + POOL_SQUARES - 1)
                        of = square_sum[:, :]
                    for i in range(QB):
                        last = pe.matmul(ps[:, 0, i:i + 1], of[:, i * P:(i + 1) * P], ones[:, 0:1],
                                         start=(at == POOL_SQUARES and i == 0), stop=(at == KT and i == QB - 1))
                last.then_inc(sum_done, 1)
                pe.wait_ge(diagonal_ready, QB)
                pe.matmul(ps[:, 1, :], ones[:, :], square_sum[:, :], start=True, stop=True).then_inc(spread_done, 1)

            def project(n, g, part=range(KT), layer=None, tokens=ALL):
                if 0 in part:
                    if above_zero(n.half):
                        pe.wait_ge(bank_read[n.slot], number(n.half))
                    pe.wait_ge(w_lo_ready, number(g + 1))
                for at in part:
                    k = M_ORDER[at]
                    if layer is not None:
                        pe.wait_ge(u_lo_ready, number(layer * KT + at + 1))
                    blk = slice(k * P, (k + 1) * P)
                    out = ps[:, n.slot, tokens]
                    pe.matmul(out, w_hi[:, g.slot, blk], u_hi[:, k, tokens], start=(at == 0), stop=False)
                    pe.matmul(out, w_hi[:, g.slot, blk], u_lo[:, k, tokens], start=False, stop=False)
                    last = pe.matmul(out, w_lo[:, g.slot, blk], u_hi[:, k, tokens], start=False,
                                     stop=(at == KT - 1))
                if KT - 1 in part:
                    last.then_inc(tile_done, 1)

            def second_project(layer, n, g, first, tokens=ALL):
                project(n, g, range(0, first), tokens=tokens)
                sum_squares(layer)
                project(n, g, range(first, KT), tokens=tokens)

            def turn_iw():
                pe.wait_ge(iwT_ready, 1)
                for i in range(1, QB):
                    last = pe.transpose(ps[:, T_BANK, (i - 1) * IDX_HEADS:i * IDX_HEADS],
                                        iwT[:, i * P:(i + 1) * P], ident[0:IDX_HEADS, 0:IDX_HEADS])
                last.then_inc(iw_turned, 1)

            def index_scores(t):
                pe.wait_ge(rope_lo_ready, number(t + (R_IQ + 1)))
                for s in range(2):
                    for kk, i in enumerate((3, 2, 1)):
                        if above_zero(t * 6 + (3 * s + kk - 5)):
                            pe.wait_ge(rel_ready, number(t * 6 + (3 * s + kk - 5)))
                        out = ps[:, (S_BANK, T_BANK)[s] + i - 1, 0:(i + 1) * P]
                        qs, ks = slice(i * P, (i + 1) * P), slice(0, (i + 1) * P)
                        pe.matmul(out, q_hi[:, t.slot, qs], ik[:, 2 * s, ks], start=True, stop=False)
                        pe.matmul(out, q_hi[:, t.slot, qs], ik[:, 2 * s + 1, ks], start=False, stop=False)
                        pe.matmul(out, q_lo[:, t.slot, qs], ik[:, 2 * s, ks], start=False,
                                  stop=True).then_inc(idx_done, 1)

            def turn_v(n):
                pe.wait_ge(bank_read[n.slot], number(n.half + 1))
                for j in range(QB):
                    last = pe.transpose(ps[:, T_BANK + 1, j * P:(j + 1) * P], v_f[:, j * P:(j + 1) * P], ident[:, :])
                last.then_inc(v_turned, 1)

            def scores(n, slot, r):
                pe.wait_ge(rope_lo_ready, number(r + 1))
                for kk, i in enumerate((3, 2, 1, 0)):
                    if above_zero(n * QB - QB + (1, 2, 4, 4)[kk]):
                        pe.wait_ge(scores_read, number(n * QB - QB + (1, 2, 4, 4)[kk]))
                    at = 2 * P if i == 0 else 0
                    out = ps[:, S_BANK + max(i, 1) - 1, at:at + (i + 1) * P]
                    qs, ks = slice(i * P, (i + 1) * P), slice(0, (i + 1) * P)
                    pe.matmul(out, q_hi[:, slot, qs], k_hi[:, ks], start=True, stop=False)
                    pe.matmul(out, q_hi[:, slot, qs], k_lo[:, ks], start=False, stop=False)
                    last = pe.matmul(out, q_lo[:, slot, qs], k_hi[:, ks], start=False, stop=True)
                    if i != 1:
                        last.then_inc(scores_done, 1)

            def turn_probs(n):
                pe.wait_ge(probs_ready, number(n * QB + QB))
                if above_zero(n):
                    pe.wait_ge(gated_ready, number(n))
                for b, js in enumerate(((0,), (1,), (2, 3))):
                    for j in js:
                        for i in range(j, QB):
                            at = T_OFF[j] - T_OFF[js[0]] + (i - j) * P
                            src = OFF[i] + j * P
                            last = pe.transpose(ps[:, T_BANK + b, at:at + P], probs[:, src:src + P], ident[:, :])
                    last.then_inc(probs_turned, 1)

            def output(n):
                for j in range(QB):
                    pe.wait_ge(pT_lo_ready, number(n * 3 + min(j, 2) + 1))
                    out = ps[:, T_BANK, j * P:SEQ]
                    vs, cols = slice(j * P, (j + 1) * P), slice(T_OFF[j], T_OFF[j] + SEQ - j * P)
                    pe.matmul(out, v_hi[:, vs], pT_hi[:, cols], start=(j == 0), stop=False)
                    pe.matmul(out, v_hi[:, vs], pT_lo[:, cols], start=False, stop=False)
                    last = pe.matmul(out, v_lo[:, vs], pT_hi[:, cols], start=False, stop=(j == QB - 1))
                last.then_inc(o_done, 1)

            def out_projection(layer, t, first=False, final=False):
                g = t + T_OUT[layer]
                pe.wait_ge(w_lo_ready, number(g + 1))
                pe.wait_ge(o_lo_ready, number(t + (layer * HEADS + 1)))
                for m in M_ORDER:
                    if first and m < 2:
                        pe.wait_ge(bank_read[m], number((PROJ_B + layer * 4 * HEADS + 1 - m) // 2))
                    if first and m == T_BANK:
                        pe.wait_ge(gated_ready, number((layer + 1) * HEADS))
                    blk = slice(m * P, (m + 1) * P)
                    pe.matmul(ps[:, m, :], w_hi[:, g.slot, blk], o_hi[:, t.slot, :], start=first, stop=False)
                    pe.matmul(ps[:, m, :], w_hi[:, g.slot, blk], o_lo[:, t.slot, :], start=False, stop=False)
                    last = pe.matmul(ps[:, m, :], w_lo[:, g.slot, blk], o_hi[:, t.slot, :], start=False, stop=final)
                    if m == M_ORDER[-1]:
                        last.then_inc(tile_done, 1)
                    elif final:
                        last.then_inc(y_done, 1)

            def out_projections(layer):
                out_projection(layer, Count(0), first=True)
                with pe.Fori(0, HEADS // 2 - 1) as i:
                    out_projection(layer, Count(1, 2, i))
                    out_projection(layer, Count(2, 2, i))
                out_projection(layer, Count(HEADS - 1), final=True)

            def head_a(h):
                attend, finish = (lo <= h.base < lo + HEADS or h.per for lo in (2, 3))
                query = h.base < HEADS + LATE_GATES or h.per
                if attend:
                    scores(h - 2, h.base % 2, h + (R_Q - 2))
                if query:
                    project(h + T_Q, h + T_Q, range(0, KT // 2))
                if finish:
                    output(h - 3)
                end = KT - 2 if h.base == HEADS + 1 and not h.per else KT
                if query:
                    project(h + T_Q, h + T_Q, range(KT // 2, end))
                if attend:
                    turn_probs(h - 2)
                if end < KT:
                    project(h + T_Q, h + T_Q, range(end, KT))

            def head_b(h):
                new, attend, last_new = h.base < HEADS or h.per, h.base > 0, h.base == HEADS - 1 and not h.per
                n, proj, tile = h + (HEADS - 1), h * 4 + PROJ_B, h * 4 + T_B
                if attend and new:
                    scores(n, 0, h * 2 + (R_B - 1))
                    project(proj - 1, tile - 1)
                if not new:
                    project(proj - 1, tile - 1, range(0, 2))
                    turn_v(proj - 2)
                    project(proj - 1, tile - 1, range(2, 6))
                if new:
                    project(proj, tile, layer=None if attend else 1)
                if not new:
                    pe.wait_ge(v_lo_ready, HEADS + 1)
                if attend:
                    turn_probs(n)
                if attend and new:
                    project(proj + 1, tile + 1)
                elif new:
                    second_project(1, proj + 1, tile + 1, 0)
                if not new:
                    project(proj - 1, tile - 1, range(6, KT))
                if new:
                    project(proj + 2, tile + 2, range(0, 5 if last_new else KT))
                if attend:
                    output(n)
                if last_new:
                    scores(n + 1, 0, h * 2 + (R_B + 1))
                    project(proj + 2, tile + 2, range(5, KT))
                if new and not last_new:
                    turn_v(proj + 2)

            pe.wait_ge(ones_ready, 1)
            project(Count(T_IK), Count(T_IK), layer=0)
            second_project(0, Count(T_IQ), Count(T_IQ), 1, CHOOSING)
            second = Count(T_IQ + 1)
            project(second, second, range(0, KT // 2), tokens=CHOOSING)
            pe.wait_ge(table_landed, 16 * 3)
            turn_iw()
            project(second, second, range(KT // 2, KT), tokens=CHOOSING)

            def idx_step(t, tokens=CHOOSING):
                project(t + T_IQ, t + T_IQ, range(0, KT // 2), tokens=tokens)
                if t.base == 2:
                    pe.wait_ge(iw_ready, 1)
                    pe.wait_ge(ik_lo_ready, 1)
                index_scores(t - 2)
                project(t + T_IQ, t + T_IQ, range(KT // 2, KT), tokens=tokens)

            idx_step(Count(2))
            idx_step(Count(3))
            with pe.Fori(0, IDX_TILES // 2 - 2) as i:
                idx_step(Count(4, 2, i))
                idx_step(Count(5, 2, i))
            idx_step(Count(IDX_TILES), ALL)
            idx_step(Count(IDX_TILES + 1), ALL)
            project(Count(T_Z), Count(T_Z))
            pe.wait_ge(rel_ready, 6 * IDX_TILES)
            turn_v(Count(T_V))
            with pe.Fori(0, (EARLY_GATES - 2) // 4) as i:
                for j in range(4):
                    n = Count(T_Z + 1 + j, 4, i)
                    project(n, n)
            project(Count(T_Q - 1), Count(T_Q - 1))
            pe.wait_ge(v_lo_ready, 1)
            for h0 in range(3):
                head_a(Count(h0))
            with pe.Fori(0, HEADS // 2 - 2) as i:
                head_a(Count(3, 2, i))
                head_a(Count(4, 2, i))
            for h0 in range(HEADS - 1, HEADS + 3):
                head_a(Count(h0))
            out_projections(0)
            pe.wait_ge(residual_ready, M_ORDER.index(PROJ_B % 2) + 1)
            head_b(Count(0))
            with pe.Fori(0, HEADS - 2) as i:
                head_b(Count(1, 1, i))
            head_b(Count(HEADS - 1))
            head_b(Count(HEADS))
            out_projections(1)
            sum_last_squares()

        @block.scalar
        def _(act):
            def split_w(g):
                act.wait_ge(w_landed[g.slot], number((g.half + 1) * 16))
                if above_zero(g - 1):
                    act.wait_ge(tile_done, number(g - 1))
                act.activation(w_hi[:, g.slot, :], w_raw[:, g.slot, :], ACT.Copy).then_inc(w_hi_ready, 1)

            def norm(layer):
                for at, m in enumerate(M_ORDER):
                    if layer == 0:
                        act.wait_ge(x_landed[m], 16)
                    else:
                        act.wait_ge(residual_ready, number((layer - 1) * KT + at + 1))
                    if layer < 2:
                        act.activation(u_hi[:, m, :], h[:, m, :], ACT.Copy,
                                       scale=gain[:, layer * KT + m:layer * KT + m + 1]).then_inc(u_hi_ready, 1)
                    if at >= SQUARES and layer < 2:
                        act.wait_ge(squares_added, number(layer * (KT - 1) + max(at - SQUARES, 1)))
                    out = square[:, at % SQUARES, :] if layer < 2 else last_square[:, at, :]
                    act.activation(out, h[:, m, :], ACT.Square).then_inc(squares_ready, 1)

            def root(out, sums, layer):
                act.wait_ge(sum_done, number(layer + 1))
                act.activation(out, sums, ACT.Sqrt, scale=1.0 / D_MODEL, bias=eps[:, 0:1]).then_inc(root_ready, 1)

            def rope_hi(r, out, tokens=ALL):
                act.wait_ge(rotated_ready, number(r + 1))
                act.activation(out, rotated[:, r.slot, tokens], ACT.Copy).then_inc(rope_hi_ready, 1)

            def relu(t):
                for s in range(2):
                    for kk, i in enumerate((3, 2, 1)):
                        act.wait_ge(idx_done, number(t * 6 + (3 * s + kk + 1)))
                        if above_zero(t * 6 + (3 * s + kk - 5)):
                            act.wait_ge(score_ready, number(t * 6 + (3 * s + kk - 5)))
                        at = OFF[i] - P
                        act.activation(rel[s][:, at:at + (i + 1) * P],
                                       ps[:, (S_BANK, T_BANK)[s] + i - 1, 0:(i + 1) * P],
                                       ACT.Relu).then_inc(rel_ready, 1)

            def v_part(vn):
                act.wait_ge(v_turned, number(vn + 1))
                act.activation(v_hi[:, :], ps[:, T_BANK + 1, :], ACT.Copy).then_inc(v_hi_ready, 1)

            def silu(z, row, n):
                act.wait_ge(bank_read[n.slot], number(n.half + 1))
                act.activation(gated[:, row.value, :], z_f[:, :], ACT.Silu).then_inc(silu_ready, 1)

            def exps(n):
                if above_zero(n * 3):
                    act.wait_ge(probs_turned, number(n * 3))
                for kk, i in enumerate((3, 2, 1, 0)):
                    act.wait_ge(scores_read, number(n * QB + (kk + 1)))
                    cols = slice(OFF[i], OFF[i] + (i + 1) * P)
                    act.activation(probs[:, cols], neg_s[:, cols], ACT.Exp, bias=neg_max[:, i:i + 1], scale=-1.0,
                                   accum_out=den[:, i:i + 1]).then_inc(exp_done, 1)

            def probs_hi(n):
                for b, (at, end) in enumerate(((0, T_OFF[1]), (T_OFF[1], T_OFF[2]), (T_OFF[2], COLS))):
                    act.wait_ge(probs_turned, number(n * 3 + (b + 1)))
                    act.activation(pT_hi[:, at:end], ps[:, T_BANK + b, 0:end - at],
                                   ACT.Copy).then_inc(pT_hi_ready, 1)

            def split_o(layer, t):
                act.wait_ge(gated_ready, number(t + (layer * HEADS + 1)))
                act.wait_ge(tile_done, number(t + (T_OUT[layer] - 1)))
                act.activation(o_hi[:, t.slot, :], gated[:, t.value, :], ACT.Copy).then_inc(o_hi_ready, 1)

            def head_a(h):
                attend, rope = (lo <= h.base < lo + HEADS or h.per for lo in (2, 1))
                if 0 < h.base < HEADS + LATE_GATES or h.per:
                    split_w(h + (T_Q + 1))
                if attend:
                    exps(h - 2)
                if rope:
                    rope_hi(h + (R_Q - 1), q_hi[:, (h.base - 1) % 2, :])
                if h.base > HEADS and not h.per:
                    silu(h - (LATE_GATES + 1), h - (LATE_GATES + 1), h + (T_Q - 1))
                if attend:
                    probs_hi(h - 2)

            def head_b(h):
                new, attend, last_new = h.base < HEADS or h.per, h.base > 0, h.base == HEADS - 1 and not h.per
                n, proj, tile, r = h + (HEADS - 1), h * 4 + PROJ_B, h * 4 + T_B, h * 2 + R_B
                if attend:
                    split_w(tile)
                if not new:
                    v_part(h)
                    split_o(1, Count(0))
                if attend and new:
                    exps(n)
                    split_w(tile + 1)
                    silu(n, h - 1, proj - 1)
                    act.preload_act_table(ACT.Exp)
                    split_w(tile + 2)
                if attend:
                    probs_hi(n)
                if not new:
                    silu(n, h - 1, proj - 1)
                if new:
                    rope_hi(r, q_hi[:, 0, :])
                    split_w(tile + 3)
                    rope_hi(r + 1, k_hi[:, :])
                if last_new:
                    exps(n + 1)
                elif new:
                    v_part(h + 1)

            def out_projections(layer):
                def step(t):
                    if t.base < HEADS - 1 or t.per:
                        split_w(t + (T_OUT[layer] + 1))
                        split_o(layer, t + 1)
                    elif layer == 0:
                        split_w(t + (T_OUT[layer] + 1))

                step(Count(0))
                with act.Fori(0, HEADS // 2 - 1) as i:
                    step(Count(1, 2, i))
                    step(Count(2, 2, i))
                step(Count(HEADS - 1))

            act.dma_start(gain[:, :], gains).then_inc(gain_landed, 16)
            act.preload_act_table(ACT.Sqrt)
            split_w(Count(0))
            act.wait_ge(gain_landed, 16)
            norm(0)
            split_w(Count(1))
            split_w(Count(2))
            act.wait_ge(eps_ready, 1)
            root(rstd[:, :], ps[:, S_BANK, :], 0)
            split_w(Count(3))
            act.wait_ge(ik_zeroed, 1)
            act.wait_ge(rotated_ready, 1)
            for s in range(2):
                for half in range(2):
                    to, of = slice(64 * half + 32 * s, 64 * half + 32 * s + 32), slice(64 * half, 64 * half + 32)
                    last = act.activation(ik[to, 2 * s, :], rotated[of, 0, :], ACT.Copy)
                last.then_inc(rope_hi_ready if s else ik_hi_ready, 1)
            rope_hi(Count(R_IQ), q_hi[:, 0, CHOOSING], CHOOSING)
            act.preload_act_table(ACT.Silu)

            def idx_step(t):
                split_w(t + (T_IQ + 1))
                if t.base <= IDX_TILES or t.per:
                    rope_hi(t + (R_IQ - 1), q_hi[:, (t.base - 1) % 2, CHOOSING], CHOOSING)
                relu(t - 2)

            idx_step(Count(2))
            with act.Fori(0, IDX_TILES // 2 - 1) as i:
                idx_step(Count(3, 2, i))
                idx_step(Count(4, 2, i))
            idx_step(Count(IDX_TILES + 1))
            act.wait_ge(score_ready, 6 * IDX_TILES)
            act.activation(left, score[:, :], ACT.Copy).then_inc(left_ready, 1)
            split_w(Count(T_Z + 1))
            rope_hi(Count(R_K), k_hi[:, :])

            def gate_step(z):
                n = z + T_Z
                split_w(n + 2)
                silu(z, z, n)

            gate_step(Count(0))
            v_part(Count(0))
            with act.Fori(0, EARLY_GATES // 2 - 1) as i:
                gate_step(Count(1, 2, i))
                gate_step(Count(2, 2, i))
            gate_step(Count(EARLY_GATES - 1))
            head_a(Count(0))
            act.preload_act_table(ACT.Exp)
            for h0 in range(1, 3):
                head_a(Count(h0))
            with act.Fori(0, HEADS // 2 - 2) as i:
                head_a(Count(3, 2, i))
                head_a(Count(4, 2, i))
            for h0 in range(HEADS - 1, HEADS + 2):
                head_a(Count(h0))
            split_o(0, Count(0))
            head_a(Count(HEADS + 2))
            out_projections(0)
            act.preload_act_table(ACT.Sqrt)
            norm(1)
            split_w(Count(T_B + 1))
            split_w(Count(T_B + 2))
            root(rstd[:, :], ps[:, S_BANK, :], 1)
            act.preload_act_table(ACT.Exp)
            head_b(Count(0))
            with act.Fori(0, HEADS - 2) as i:
                head_b(Count(1, 1, i))
            head_b(Count(HEADS - 1))
            head_b(Count(HEADS))
            out_projections(1)
            act.preload_act_table(ACT.Sqrt)
            norm(2)
            root(root_turned[:, :], ps[:, 0, 0:QB], 2)

        @block.vector
        def _(dve):
            def norm(layer):
                for at, m in enumerate(M_ORDER):
                    if layer:
                        if at < KT - 1:
                            dve.wait_ge(y_done, number((layer - 1) * (KT - 1) + at + 1))
                        else:
                            dve.wait_ge(tile_done, number(T_OUT[layer - 1] + HEADS))
                        dve.tensor_tensor(h[:, m, :], ps[:, m, :], h[:, m, :], ALU.add).then_inc(residual_ready, 1)
                    if layer < 2 and at:
                        u_part(layer, at - 1)
                if layer < 2:
                    u_part(layer, KT - 1)

            def u_part(layer, at):
                m = M_ORDER[at]
                dve.wait_ge(u_hi_ready, number(layer * KT + at + 1))
                dve.scalar_tensor_tensor(out=u_lo[:, m, :], in0=h[:, m, :],
                                         scalar=gain[:, layer * KT + m:layer * KT + m + 1],
                                         in1=u_hi[:, m, :].bitcast(F32), op0=ALU.mult,
                                         op1=ALU.subtract).then_inc(u_lo_ready, 1)

            def split_w(g):
                dve.wait_ge(w_hi_ready, number(g + 1))
                dve.tensor_tensor(w_lo[:, g.slot, :], w_raw[:, g.slot, :], w_hi[:, g.slot, :].bitcast(F32),
                                  ALU.subtract).then_inc(w_lo_ready, 1)

            def invert_root(layer):
                dve.wait_ge(root_ready, number(layer + 1))
                dve.reciprocal(rstd[:, :], rstd[:, :]).then_inc(rstd_ready, 1)
                dve.wait_ge(rstd_ready, number(layer + 1))

            def scale_tables(layer):
                for s in range(2):
                    dve.tensor_tensor(scaled[:, s, :], table[:, s, :], rstd[:, :], ALU.mult).then_inc(tables_scaled, 1)
                dve.wait_ge(tables_scaled, number(2 * layer + 2))

            def scale_values(n, g):
                dve.wait_ge(tile_done, number(g + 1))
                dve.tensor_tensor(v_f[:, :], ps[:, n.slot, :], rstd[:, :], ALU.mult).then_inc(bank_read[n.slot], 1)

            def scale_gate(z, n, g):
                dve.wait_ge(tile_done, number(g + 1))
                if above_zero(z):
                    dve.wait_ge(silu_ready, number(z))
                dve.tensor_tensor(z_f[:, :], ps[:, n.slot, :], rstd[:, :], ALU.mult).then_inc(bank_read[n.slot], 1)

            def first_rope(n, g, cos):
                dve.wait_ge(tile_done, number(g + 1))
                half = P // 2
                dve.tensor_tensor(by_sin[0:half, :], ps[half:P, n.slot, :], table[half:P, cos + 1, :], ALU.mult)
                dve.tensor_tensor(by_sin[half:P, :], ps[0:half, n.slot, :], table[0:half, cos + 1, :], ALU.mult)
                dve.tensor_tensor(by_cos[:, :], ps[:, n.slot, :], table[:, cos, :], ALU.mult).then_inc(
                    bank_read[n.slot], 1)
                dve.wait_ge(bank_read[n.slot], number(n.half + 1))
                dve.tensor_tensor(rotated[:, 0, :], by_cos[:, :], by_sin[:, :], ALU.add).then_inc(first_ready, 1)

            def scale_first(layer):
                dve.wait_ge(first_ready, layer + 1)
                dve.tensor_tensor(rotated[:, 0, :], rotated[:, 0, :], rstd[:, :], ALU.mult).then_inc(rotated_ready, 1)

            def rope(r, n, g, of=scaled, cos=0, tokens=ALL):
                dve.wait_ge(tile_done, number(g + 1))
                if above_zero(r):
                    dve.wait_ge(rotated_ready, number(r))
                raw, half = ps[:, n.slot, tokens], P // 2
                for out, other in ((slice(0, half), slice(half, P)), (slice(half, P), slice(0, half))):
                    dve.tensor_tensor(by_sin[out, tokens], ps[other, n.slot, tokens], of[other, cos + 1, tokens],
                                      ALU.mult)
                dve.tensor_tensor(by_cos[:, tokens], raw, of[:, cos, tokens], ALU.mult).then_inc(bank_read[n.slot], 1)
                dve.wait_ge(bank_read[n.slot], number(n.half + 1))
                if above_zero(r - 1):
                    dve.wait_ge(rope_lo_ready, number(r - 1))
                dve.tensor_tensor(rotated[:, r.slot, tokens], by_cos[:, tokens], by_sin[:, tokens],
                                  ALU.add).then_inc(rotated_ready, 1)

            def add_scores(t):
                for s in range(2):
                    for kk, i in enumerate((3, 2, 1)):
                        dve.wait_ge(rel_ready, number(t * 6 + (3 * s + kk + 1)))
                        if above_zero(t * 6 + (3 * s + kk - 2)):
                            dve.wait_ge(score_ready, number(t * 6 + (3 * s + kk - 2)))
                        cols = slice(OFF[i] - P, OFF[i] + i * P)
                        head = (t * 2 + s).value
                        dve.scalar_tensor_tensor(out=score[:, cols], in0=rel[s][:, cols],
                                                 scalar=iw[:, i - 1, bass.ds(head, 1)], in1=score[:, cols],
                                                 op0=ALU.mult, op1=ALU.add).then_inc(score_ready, 1)

            def take_eight(r):
                for i in range(1, QB):
                    if above_zero(r * 3 + (i - 3)):
                        least = in_register(dve, r * 3 + (i - 3))
                        dve.wait_ge(top8_taken, 1)
                        dve.wait_ge(top8_taken, least)
                    dve.max(top8[:, i - 1, :], left[:, OFF[i] - P:OFF[i] + i * P]).then_inc(top8_ready, 1)
                for i in range(1, QB):
                    least = in_register(dve, r * 3 + i)
                    dve.wait_ge(top8_ready, 1)
                    dve.wait_ge(top8_ready, least)
                    part = left[:, OFF[i] - P:OFF[i] + i * P]
                    dve.match_replace(part, top8[:, i - 1, :], part, NEG).then_inc(top8_taken, 1)

            def mask_scores(n, bias, offset):
                for kk, i in enumerate((3, 2, 1, 0)):
                    if i:
                        if above_zero(n * QB + (kk + 1 - QB)):
                            dve.wait_ge(exp_done, number(n * QB + (kk + 1 - QB)))
                        least = in_register(dve, n * 3 + (kk + 1))
                        dve.wait_ge(scores_done, 1)
                        dve.wait_ge(scores_done, least)
                    else:
                        if above_zero(n * QB):
                            least = in_register(dve, n * QB)
                            dve.wait_ge(exp_done, 1)
                            dve.wait_ge(exp_done, least)
                    at = 2 * P if i == 0 else 0
                    width = (i + 1) * P
                    dve.tensor_tensor_reduce(neg_s[:, OFF[i]:OFF[i] + width],
                                             ps[:, S_BANK + max(i, 1) - 1, at:at + width],
                                             bias[:, offset(i):offset(i) + width], -SCALE, -NEG, ALU.add, ALU.min,
                                             neg_max[:, i:i + 1]).then_inc(scores_read, 1)

            def invert(n):
                dve.wait_ge(exp_done, number(n * QB + QB))
                dve.reciprocal(inv_den[:, :], den[:, :]).then_inc(inv_ready, 1)

            def probs_lo(n):
                for b, (at, end) in enumerate(((0, T_OFF[1]), (T_OFF[1], T_OFF[2]), (T_OFF[2], COLS))):
                    dve.wait_ge(pT_hi_ready, number(n * 3 + (b + 1)))
                    dve.tensor_tensor(pT_lo[:, at:end], ps[:, T_BANK + b, 0:end - at],
                                      pT_hi[:, at:end].bitcast(F32), ALU.subtract).then_inc(pT_lo_ready, 1)

            def v_part(vn):
                dve.wait_ge(v_hi_ready, number(vn + 1))
                dve.tensor_tensor(v_lo[:, :], ps[:, T_BANK + 1, :], v_hi[:, :].bitcast(F32),
                                  ALU.subtract).then_inc(v_lo_ready, 1)

            def gate(n, row):
                dve.wait_ge(o_done, number(n + 1))
                dve.wait_ge(silu_ready, number(n + 1))
                dve.tensor_tensor(gated[:, row.value, :], ps[:, T_BANK, :], gated[:, row.value, :],
                                  ALU.mult).then_inc(gated_ready, 1)

            def split_o(layer, t):
                dve.wait_ge(o_hi_ready, number(t + (layer * HEADS + 1)))
                dve.tensor_tensor(o_lo[:, t.slot, :], gated[:, t.value, :], o_hi[:, t.slot, :].bitcast(F32),
                                  ALU.subtract).then_inc(o_lo_ready, 1)

            def out_projections(layer):
                with dve.Fori(0, HEADS // 2 - 1) as i:
                    split_o(layer, Count(1, 2, i))
                    split_o(layer, Count(2, 2, i))
                split_o(layer, Count(HEADS - 1))

            def head_a(h):
                attend, roped, finish = (lo <= h.base < lo + HEADS or h.per for lo in (2, 1, 3))
                if attend:
                    mask_scores(h - 2, bias_a, lambda i: OFF[i])
                if roped:
                    rope(h + (R_Q - 1), h + (T_Q - 1), h + (T_Q - 1))
                if attend:
                    invert(h - 2)
                if h.base > HEADS and not h.per:
                    scale_gate(h - (LATE_GATES + 1), h + (T_Q - 1), h + (T_Q - 1))
                if finish:
                    gate(h - 3, h - 3)
                if attend:
                    probs_lo(h - 2)

            def head_b(h):
                new, attend, last_new = h.base < HEADS or h.per, h.base > 0, h.base == HEADS - 1 and not h.per
                n, proj, tile, r = h + (HEADS - 1), h * 4 + PROJ_B, h * 4 + T_B, h * 2 + R_B
                if attend and new:
                    mask_scores(n, bias_b, lambda i: SEQ - (i + 1) * P)
                    invert(n)
                    scale_gate(n, proj - 1, tile - 1)
                    rope(r, proj, tile)
                if not new:
                    split_o(1, Count(0))
                if attend:
                    probs_lo(n)
                if not new:
                    scale_gate(n, proj - 1, tile - 1)
                if new:
                    rope(r + 1, proj + 1, tile + 1)
                if last_new:
                    gate(n, h - 1)
                    mask_scores(n + 1, bias_b, lambda i: SEQ - (i + 1) * P)
                if new:
                    scale_values(proj + 2, tile + 2)
                if last_new:
                    invert(n + 1)
                if attend and not last_new:
                    gate(n, h - 1)
                if new:
                    v_part(h + 1)

            dve.memset(ones[:, :], 1.0).then_inc(ones_ready, 1)
            dve.memset(eps[:, :], NORM_EPS).then_inc(eps_ready, 1)
            split_w(Count(0))
            dve.wait_ge(gain_landed, 16)
            norm(0)
            split_w(Count(1))
            dve.wait_ge(tile_done, 1)
            dve.tensor_scalar(iwT[:, :], ps[32:32 + IDX_HEADS, 0, :], IDX_SCALE, None, ALU.mult).then_inc(iwT_raw, 1)
            dve.wait_ge(table_landed, 16 * 3)
            first_rope(Count(0), Count(0), cos=2)
            invert_root(0)
            dve.wait_ge(iwT_raw, 1)
            dve.tensor_tensor(iwT[:, :], iwT[:, :], rstd[0:IDX_HEADS, :], ALU.mult).then_inc(iwT_ready, 1)
            scale_first(0)
            for s in range(2):
                dve.tensor_tensor(table[:, 2 + s, :], table[:, 2 + s, :], rstd[:, :], ALU.mult).then_inc(idx_scaled, 1)
            dve.wait_ge(idx_scaled, 2)
            rope(Count(R_IQ), Count(T_IQ), Count(T_IQ), of=table, cos=2, tokens=CHOOSING)
            dve.wait_ge(iw_turned, 1)
            dve.tensor_copy(iw[:, :, :], ps[:, T_BANK, 0:(QB - 1) * IDX_HEADS].rearrange(
                "p (i n) -> p i n", n=IDX_HEADS)).then_inc(iw_ready, 1)
            dve.wait_ge(ik_hi_ready, 1)
            for half in range(2):
                part = slice(64 * half, 64 * half + 32)
                last = dve.tensor_tensor(ik[part, 1, :], rotated[part, 0, :], ik[part, 0, :].bitcast(F32),
                                         ALU.subtract)
            last.then_inc(ik_lo_ready, 1)
            dve.wait_ge(iw_ready, 1)
            dve.wait_ge(score_zeroed, 2)
            dve.wait_ge(rope_hi_ready, 1)

            def idx_step(t):
                rope(t + (R_IQ - 1), t + (T_IQ - 1), t + (T_IQ - 1), of=table, cos=2, tokens=CHOOSING)
                add_scores(t - 2)

            idx_step(Count(2))
            with dve.Fori(0, IDX_TILES // 2 - 1) as i:
                idx_step(Count(3, 2, i))
                idx_step(Count(4, 2, i))
            scale_values(Count(T_V), Count(T_V))
            add_scores(Count(IDX_TILES - 1))
            scale_tables(0)
            rope(Count(R_K), Count(T_K), Count(T_K))
            dve.wait_ge(left_ready, 1)
            take_eight(Count(0))

            def gate_step(z):
                scale_gate(z, z + T_Z, z + T_Z)
                take_eight(z + 1)

            gate_step(Count(0))
            v_part(Count(0))
            with dve.Fori(0, EARLY_GATES // 2 - 1) as i:
                gate_step(Count(1, 2, i))
                gate_step(Count(2, 2, i))
            gate_step(Count(EARLY_GATES - 1))
            for r in range(EARLY_GATES + 1, TOP_K // 8):
                take_eight(Count(r))
            for h0 in range(2):
                head_a(Count(h0))
            dve.wait_ge(top8_taken, 3 * TOP_K // 8)
            dve.tensor_tensor(bias_a[:, P:COLS], score[:, :], left, ALU.is_gt).then_inc(chosen_ready, 1)
            dve.wait_ge(chosen_ready, 1)
            dve.tensor_scalar(bias_a[:, P:COLS], bias_a[:, P:COLS], -1.0, -NEG, ALU.add,
                              ALU.mult).then_inc(bias_ready, 1)
            dve.wait_ge(bias_ready, 1)
            dve.wait_ge(bias_landed, 32)
            head_a(Count(2))
            with dve.Fori(0, HEADS // 2 - 2) as i:
                head_a(Count(3, 2, i))
                head_a(Count(4, 2, i))
            for h0 in range(HEADS - 1, HEADS + 2):
                head_a(Count(h0))
            split_o(0, Count(0))
            head_a(Count(HEADS + 2))
            out_projections(0)
            norm(1)
            split_w(Count(T_B + 1))
            first_rope(Count(PROJ_B), Count(T_B), cos=0)
            invert_root(1)
            scale_first(1)
            scale_tables(1)
            head_b(Count(0))
            with dve.Fori(0, HEADS - 2) as i:
                head_b(Count(1, 1, i))
            head_b(Count(HEADS - 1))
            head_b(Count(HEADS))
            out_projections(1)
            norm(2)
            dve.wait_ge(root_ready, 3)
            dve.reciprocal(inv_turned[:, :], root_turned[:, :]).then_inc(inv_turned_ready, 1)
            dve.wait_ge(inv_turned_ready, 1)
            for i in range(QB):
                dve.tensor_scalar(square_sum[:, i * P:(i + 1) * P], ident[:, :], inv_turned[:, i:i + 1], None,
                                  ALU.mult).then_inc(diagonal_ready, 1)
            dve.wait_ge(spread_done, 1)
            for at, m in enumerate(M_ORDER):
                if at not in POOL_OUT:
                    dve.scalar_tensor_tensor(out=h[:, m, :], in0=h[:, m, :], scalar=gain[:, 2 * KT + m:2 * KT + m + 1],
                                             in1=ps[:, 1, :], op0=ALU.mult, op1=ALU.mult).then_inc(out_dve, 1)
                if at == 0:
                    dve.tensor_copy(rstd[:, :], ps[:, 1, :]).then_inc(rstd_ready, 1)

        @block.gpsimd
        def _(pool):
            def split_w(g):
                pool.wait_ge(w_hi_ready, number(g + 1))
                pool.tensor_tensor(w_lo[:, g.slot, :], w_raw[:, g.slot, :], w_hi[:, g.slot, :].bitcast(F32),
                                   ALU.subtract).then_inc(w_lo_ready, 1)

            def add_squares(layer):
                for at in range(1, KT if layer < 2 else POOL_SQUARES):
                    pool.wait_ge(squares_ready, number(layer * KT + at + 1))
                    if at > 1:
                        pool.wait_ge(squares_added, number(layer * (KT - 1) + at - 1))
                    new = square[:, at % SQUARES, :] if layer < 2 else last_square[:, at, :]
                    first = square[:, 0, :] if layer < 2 else last_square[:, 0, :]
                    pool.tensor_tensor(square_sum[:, :], first if at == 1 else square_sum[:, :], new,
                                       ALU.add).then_inc(squares_added, 1)

            def rope_lo(r, hi, lo, tokens=ALL):
                pool.wait_ge(rope_hi_ready, number(r + 1))
                pool.tensor_tensor(lo, rotated[:, r.slot, tokens], hi.bitcast(F32),
                                   ALU.subtract).then_inc(rope_lo_ready, 1)

            def normalise(n):
                least = in_register(pool, n + 1)
                pool.wait_ge(inv_ready, 1)
                pool.wait_ge(inv_ready, least)
                for i in (3, 2, 1, 0):
                    cols = slice(OFF[i], OFF[i] + (i + 1) * P)
                    pool.tensor_scalar(probs[:, cols], probs[:, cols], inv_den[:, i:i + 1], 1.0, ALU.mult,
                                       ALU.mult).then_inc(probs_ready, 1)

            def head_a(h):
                attend, rope = (lo <= h.base < lo + HEADS or h.per for lo in (2, 1))
                if h.base < HEADS + LATE_GATES or h.per:
                    split_w(h + (T_Q + 1))
                if attend:
                    normalise(h - 2)
                if rope:
                    slot = (h.base - 1) % 2
                    rope_lo(h + (R_Q - 1), q_hi[:, slot, :], q_lo[:, slot, :])

            def head_b(h):
                new, attend = h.base < HEADS or h.per, h.base > 0
                tile, r = h * 4 + T_B, h * 2 + R_B
                if attend and new:
                    split_w(tile)
                    normalise(h + (HEADS - 1))
                elif attend:
                    normalise(h + (HEADS - 1))
                    split_w(tile)
                if attend and new:
                    split_w(tile + 1)
                if new:
                    split_w(tile + 2)
                    rope_lo(r, q_hi[:, 0, :], q_lo[:, 0, :])
                    split_w(tile + 3)
                    rope_lo(r + 1, k_hi[:, :], k_lo[:, :])

            def out_projections(layer):
                def step(t):
                    if t.base < HEADS - 1 or t.per or layer == 0:
                        split_w(t + (T_OUT[layer] + 1))

                step(Count(0))
                with pool.Fori(0, HEADS // 2 - 1) as i:
                    step(Count(1, 2, i))
                    step(Count(2, 2, i))
                step(Count(HEADS - 1))

            pool.memset(ik[:, :, :].bitcast(F32), 0.0).then_inc(ik_zeroed, 1)
            pool.memset(score[:, :], 0.0).then_inc(score_zeroed, 1)
            add_squares(0)
            pool.wait_ge(score_zeroed, 1)
            pool.wait_ge(bias_landed, 32)
            for i in range(1, QB):
                last = pool.tensor_copy(score[:, OFF[i] - P + i * P:OFF[i] + i * P], bias_a[:, 0:P])
            last.then_inc(score_zeroed, 1)

            def idx_step(t):
                split_w(t + (T_IQ + 1))
                slot = (t.base - 1) % 2
                rope_lo(t + (R_IQ - 1), q_hi[:, slot, CHOOSING], q_lo[:, slot, CHOOSING], CHOOSING)

            pool.wait_ge(w_lo_ready, 2)
            split_w(Count(T_IQ + 1))
            split_w(Count(T_IQ + 2))
            pool.wait_ge(ik_hi_ready, 1)
            pool.wait_ge(w_lo_ready, 4)
            for half in range(2):
                of = slice(64 * half, 64 * half + 32)
                last = pool.tensor_tensor(ik[64 * half + 32:64 * half + 64, 3, :], rotated[of, 0, :],
                                          ik[of, 0, :].bitcast(F32), ALU.subtract)
            last.then_inc(rope_lo_ready, 1)
            pool.wait_ge(rope_lo_ready, 1)
            rope_lo(Count(R_IQ), q_hi[:, 0, CHOOSING], q_lo[:, 0, CHOOSING], CHOOSING)
            with pool.Fori(0, IDX_TILES // 2 - 1) as i:
                idx_step(Count(2, 2, i))
                idx_step(Count(3, 2, i))
            idx_step(Count(IDX_TILES))
            split_w(Count(T_Z))
            split_w(Count(T_Z + 1))
            rope_lo(Count(R_K), k_hi[:, :], k_lo[:, :])
            with pool.Fori(0, EARLY_GATES // 2 - 1) as i:
                split_w(Count(T_Z + 2, 2, i))
                split_w(Count(T_Z + 3, 2, i))
            split_w(Count(T_Q))
            for h0 in range(3):
                head_a(Count(h0))
            with pool.Fori(0, HEADS // 2 - 2) as i:
                head_a(Count(3, 2, i))
                head_a(Count(4, 2, i))
            for h0 in range(HEADS - 1, HEADS + 3):
                head_a(Count(h0))
            out_projections(0)
            add_squares(1)
            pool.wait_ge(w_lo_ready, T_B + 2)
            head_b(Count(0))
            with pool.Fori(0, HEADS - 2) as i:
                head_b(Count(1, 1, i))
            head_b(Count(HEADS - 1))
            head_b(Count(HEADS))
            out_projections(1)
            add_squares(2)
            pool.wait_ge(rstd_ready, 3)
            for m in (M_ORDER[at] for at in POOL_OUT):
                pool.tensor_tensor(h[:, m, :], h[:, m, :], rstd[:, :], ALU.mult).then_inc(out_half, 1)
                pool.wait_ge(out_half, POOL_OUT.index(M_ORDER.index(m)) + 1)
                pool.tensor_scalar(h[:, m, :], h[:, m, :], gain[:, 2 * KT + m:2 * KT + m + 1], 1.0, ALU.mult,
                                   ALU.mult).then_inc(out_pool, 1)


def rotary_table(rows_per_head, sin):
    dim = 2 * rows_per_head
    freqs = np.float32(10000.0) ** (-np.arange(0, dim, 2, dtype=np.float32) / np.float32(dim))
    angle = np.arange(SEQ, dtype=np.float32)[None, :] * freqs[np.arange(P) % rows_per_head][:, None]
    if not sin:
        return np.cos(angle)
    return np.sin(angle) * np.where(np.arange(P) < P // 2, 1, -1).astype(np.float32)[:, None]


def constants():
    dist = np.arange(P)[:, None] - (np.arange(SEQ)[None, :] - (SEQ - P))
    times = sum(((dist >= 0) & (dist <= window) & (dist % dilation == 0)).astype(np.float64)
                for window, dilation in CONFIGS)
    dilated = np.where(times > 0, np.log(np.maximum(times, 1)) / SCALE, NEG).astype(np.float32)
    causal = np.where(np.arange(P)[:, None] >= np.arange(P)[None, :], 0, NEG).astype(np.float32)
    tables = np.stack([rotary_table(64, False), rotary_table(64, True), rotary_table(32, False),
                       rotary_table(32, True)], 1)
    return tables.astype(np.float32), dilated, causal, np.eye(P, dtype=np.float32)


def tiles_of(w):
    n = w.shape[1] // P
    return w.reshape(KT, P, n, P).transpose(2, 1, 0, 3).reshape(n, P, D_MODEL)


def kernel(**inputs):
    from concourse import bacc
    from concourse.bass_utils import run_bass_kernel_spmd

    a_in, b_in = np.asarray(inputs["a_w_in"])[0], np.asarray(inputs["b_w_in"])[0]
    ends = np.cumsum([D_INNER, HEAD_DIM, HEAD_DIM, IDX_HEADS * IDX_DIM, IDX_DIM, IDX_HEADS])
    aq, ak, av, aiq, aik, aiw, az = np.split(a_in, ends, axis=1)
    half = IDX_DIM // 2
    first = np.zeros((D_MODEL, P), a_in.dtype)
    first[:, 0:half], first[:, 64:64 + half] = aik[:, :half], aik[:, half:]
    first[:, half:half + IDX_HEADS] = aiw
    aiq = aiq.reshape(D_MODEL, IDX_TILES, 2, 2, half).transpose(0, 1, 3, 2, 4).reshape(D_MODEL, IDX_HEADS * IDX_DIM)
    b_in = b_in.reshape(D_MODEL, 4, HEADS, HEAD_DIM).transpose(0, 2, 1, 3).reshape(D_MODEL, 4 * D_INNER)
    weights = np.concatenate(
        [tiles_of(first), tiles_of(aiq), tiles_of(av), tiles_of(ak), tiles_of(az)[:EARLY_GATES], tiles_of(aq),
         tiles_of(az)[EARLY_GATES:], np.asarray(inputs["a_w_out"])[0].reshape(HEADS, P, D_MODEL), tiles_of(b_in),
         np.asarray(inputs["b_w_out"])[0].reshape(HEADS, P, D_MODEL)])
    gains = np.concatenate([np.asarray(inputs["norm_g"]), np.asarray(inputs["final_g"])[None]])
    gains = gains.reshape(3, KT, P).transpose(2, 0, 1).reshape(P, 3 * KT)
    tables, dilated, causal, ident = constants()
    arrays = {
        "x_turned": np.asarray(inputs["x"])[0].T, "gains": gains, "weights": weights, "rope_tables": tables,
        "dilated_bias": dilated, "causal_bias": causal, "identity": ident,
    }
    arrays = {name: np.ascontiguousarray(a) for name, a in arrays.items()}
    nc = bacc.Bacc("TRN2", target_bir_lowering=False, num_devices=1)
    args = [nc.dram_tensor(name, a.shape, mybir.dt.from_np(a.dtype), kind="ExternalInput").ap()
            for name, a in arrays.items()]
    args.append(nc.dram_tensor("outT", (D_MODEL, SEQ), F32, kind="ExternalOutput").ap())
    build(nc, *args)
    r = run_bass_kernel_spmd(nc, [arrays], core_ids=[0])
    return np.asarray(r.results[0]["outT"]).T.reshape(1, SEQ, D_MODEL)
```
